# Optimizing a Trainium2 kernel written in Bass

```python
import math
import jax, jax.numpy as jnp
from jax import lax
import numpy as np

D_MODEL = 1024
BATCH = 1
SEQ = 1024
DEPTH = 2

N_A_LAYERS = DEPTH // 2
N_B_LAYERS = DEPTH - N_A_LAYERS

A_HEADS = 8
A_HEAD_DIM = 64
A_INNER = A_HEADS * 2 * A_HEAD_DIM
B_HEADS = 16
B_KV_HEADS = 2
B_HEAD_DIM = 64
B_GROUP = B_HEADS // B_KV_HEADS
B_INNER = B_HEADS * B_HEAD_DIM
WINDOW = 128
Q_BLOCK = 128
EPS = 1e-6
ADA_STD = 0.02

kernel_name = "yoco_diffattn_swa_sink_hybrid"

def rms_norm(x, g):
    x32 = x.astype(jnp.float32)
    y = x32 * lax.rsqrt(jnp.mean(x32 * x32, axis=-1, keepdims=True) + EPS)
    return (y * g.astype(jnp.float32)).astype(x.dtype)

def alibi_slopes(n_heads):
    return jnp.asarray(np.array([2.0 ** (-8.0 * (h + 1) / n_heads) for h in range(n_heads)], dtype=np.float32))

def ada_modulation(c, w, b, n_chunks):
    m = jax.nn.silu(c) @ w + b
    return jnp.split(m[:, None, :], n_chunks, axis=-1)

def diff_causal_attention(q, k, v, lam, slopes):
    bsz, seq = q.shape[0], q.shape[1]
    nb = seq // Q_BLOCK
    scale = A_HEAD_DIM ** -0.5
    qb = jnp.moveaxis(q.reshape(bsz, nb, Q_BLOCK, 2 * A_HEADS, A_HEAD_DIM), 1, 0)
    kpos = jnp.arange(seq)
    sub_slopes = jnp.repeat(slopes, 2)[:, None, None]
    lam = lam.astype(jnp.float32)

    def block(args):
        qi, blk = args
        qpos = blk * Q_BLOCK + jnp.arange(Q_BLOCK)
        dist = (qpos[:, None] - kpos[None, :]).astype(jnp.float32)
        s = jnp.einsum('bqhd,bkhd->bhqk', qi, k).astype(jnp.float32) * scale - sub_slopes * dist
        s = jnp.where(dist >= 0, s, -jnp.inf)
        p = jax.nn.softmax(s, axis=-1).reshape(bsz, A_HEADS, 2, Q_BLOCK, seq)
        a = (p[:, :, 0] - lam * p[:, :, 1]).astype(v.dtype)
        return jnp.einsum('bhqk,bkhe->bqhe', a, v)

    o = lax.map(block, (qb, jnp.arange(nb)))
    return jnp.moveaxis(o, 0, 1).reshape(bsz, seq, A_HEADS, 2 * A_HEAD_DIM)

def sliding_window_sink_attention(q, k, v, sinks, slopes):
    bsz, seq = q.shape[0], q.shape[1]
    nb = seq // WINDOW
    scale = B_HEAD_DIM ** -0.5
    qb = q.reshape(bsz, nb, WINDOW, B_KV_HEADS, B_GROUP, B_HEAD_DIM)

    def band(t):
        tb = t.reshape(bsz, nb, WINDOW, B_KV_HEADS, B_HEAD_DIM)
        prev = jnp.concatenate([jnp.zeros_like(tb[:, :1]), tb[:, :-1]], axis=1)
        return jnp.concatenate([prev, tb], axis=2)

    kw, vw = band(k), band(v)
    s = jnp.einsum('bnqkgd,bnskd->bnkgqs', qb, kw).astype(jnp.float32) * scale
    dist = jnp.arange(WINDOW)[:, None] - jnp.arange(2 * WINDOW)[None, :] + WINDOW
    kpos = jnp.arange(nb)[:, None] * WINDOW + jnp.arange(2 * WINDOW)[None, :] - WINDOW
    valid = (dist >= 0) & (dist < WINDOW) & (kpos[:, None, :] >= 0)
    s = s - slopes.reshape(B_KV_HEADS, B_GROUP, 1, 1) * dist.astype(jnp.float32)
    s = jnp.where(valid[:, None, None], s, -jnp.inf)
    sink = sinks.astype(jnp.float32).reshape(1, 1, B_KV_HEADS, B_GROUP, 1)
    m = jnp.maximum(jnp.max(s, axis=-1), sink)
    e = jnp.exp(s - m[..., None])
    p = e / (jnp.sum(e, axis=-1) + jnp.exp(sink - m))[..., None]
    o = jnp.einsum('bnkgqs,bnskd->bnqkgd', p.astype(v.dtype), vw)
    return o.reshape(bsz, seq, B_HEADS, B_HEAD_DIM)

def setup_inputs(seed: int = 0) -> dict:
    key = jax.random.key(seed)
    ks = iter(jax.random.split(key, 32))
    nrm = lambda shape, std: std * jax.random.normal(next(ks), shape, dtype=jnp.float32)
    gain = lambda shape: 1.0 + nrm(shape, 0.02)
    d = D_MODEL
    kv_width = 2 * B_KV_HEADS * B_HEAD_DIM
    return {
        "x": nrm((BATCH, SEQ, d), 1.0),
        "c": nrm((BATCH, d), 1.0),
        "a_norm_g": gain((N_A_LAYERS, d)),
        "a_ada_w": nrm((N_A_LAYERS, d, 3 * d), ADA_STD),
        "a_ada_b": nrm((N_A_LAYERS, 3 * d), 0.02),
        "a_w_in": nrm((N_A_LAYERS, d, 4 * A_INNER), d ** -0.5),
        "a_q_norm_g": gain((N_A_LAYERS, A_HEAD_DIM)),
        "a_k_norm_g": gain((N_A_LAYERS, A_HEAD_DIM)),
        "a_lambda_q1": nrm((N_A_LAYERS, A_HEAD_DIM), 0.1),
        "a_lambda_k1": nrm((N_A_LAYERS, A_HEAD_DIM), 0.1),
        "a_lambda_q2": nrm((N_A_LAYERS, A_HEAD_DIM), 0.1),
        "a_lambda_k2": nrm((N_A_LAYERS, A_HEAD_DIM), 0.1),
        "a_subln_g": gain((N_A_LAYERS, 2 * A_HEAD_DIM)),
        "a_w_out": nrm((N_A_LAYERS, A_INNER, d), A_INNER ** -0.5),
        "kv_norm_g": gain((d,)),
        "kv_ada_w": nrm((d, 2 * d), ADA_STD),
        "kv_ada_b": nrm((2 * d,), 0.02),
        "w_kv": nrm((d, kv_width), d ** -0.5),
        "kv_k_norm_g": gain((B_HEAD_DIM,)),
        "b_norm_g": gain((N_B_LAYERS, d)),
        "b_ada_w": nrm((N_B_LAYERS, d, 3 * d), ADA_STD),
        "b_ada_b": nrm((N_B_LAYERS, 3 * d), 0.02),
        "b_w_in": nrm((N_B_LAYERS, d, 2 * B_INNER), d ** -0.5),
        "b_q_norm_g": gain((N_B_LAYERS, B_HEAD_DIM)),
        "b_sinks": nrm((N_B_LAYERS, B_HEADS), 0.5),
        "b_w_out": nrm((N_B_LAYERS, B_INNER, d), B_INNER ** -0.5),
    }

def reference(x, c, a_norm_g, a_ada_w, a_ada_b, a_w_in, a_q_norm_g, a_k_norm_g,
              a_lambda_q1, a_lambda_k1, a_lambda_q2, a_lambda_k2, a_subln_g, a_w_out,
              kv_norm_g, kv_ada_w, kv_ada_b, w_kv, kv_k_norm_g,
              b_norm_g, b_ada_w, b_ada_b, b_w_in, b_q_norm_g, b_sinks, b_w_out):
    bsz, seq, _ = x.shape
    slopes_a = alibi_slopes(A_HEADS)
    slopes_b = alibi_slopes(B_HEADS)
    h = x
    k_s = v_s = None
    for layer in range(DEPTH):
        if layer < N_A_LAYERS:
            l = layer
            shift, scale, gate = ada_modulation(c, a_ada_w[l], a_ada_b[l], 3)
            u = rms_norm(h, a_norm_g[l]) * (1 + scale) + shift
            q, k, v, z = jnp.split(u @ a_w_in[l], 4, axis=-1)
            q = rms_norm(q.reshape(bsz, seq, 2 * A_HEADS, A_HEAD_DIM), a_q_norm_g[l])
            k = rms_norm(k.reshape(bsz, seq, 2 * A_HEADS, A_HEAD_DIM), a_k_norm_g[l])
            v = v.reshape(bsz, seq, A_HEADS, 2 * A_HEAD_DIM)
            lambda_init = 0.8 - 0.6 * math.exp(-0.3 * l)
            lam = (jnp.exp(jnp.sum(a_lambda_q1[l].astype(jnp.float32) * a_lambda_k1[l].astype(jnp.float32)))
                   - jnp.exp(jnp.sum(a_lambda_q2[l].astype(jnp.float32) * a_lambda_k2[l].astype(jnp.float32)))
                   + lambda_init)
            o = diff_causal_attention(q, k, v, lam, slopes_a)
            o = rms_norm(o, a_subln_g[l]) * (1.0 - lambda_init)
            o = o.reshape(bsz, seq, A_INNER) * jax.nn.silu(z)
            h = h + gate * (o @ a_w_out[l])
            if layer == N_A_LAYERS - 1:
                kv_shift, kv_scale = ada_modulation(c, kv_ada_w, kv_ada_b, 2)
                ukv = rms_norm(h, kv_norm_g) * (1 + kv_scale) + kv_shift
                k_s, v_s = jnp.split(ukv @ w_kv, 2, axis=-1)
                k_s = rms_norm(k_s.reshape(bsz, seq, B_KV_HEADS, B_HEAD_DIM), kv_k_norm_g)
                v_s = v_s.reshape(bsz, seq, B_KV_HEADS, B_HEAD_DIM)
        else:
            l = layer - N_A_LAYERS
            shift, scale, gate = ada_modulation(c, b_ada_w[l], b_ada_b[l], 3)
            u = rms_norm(h, b_norm_g[l]) * (1 + scale) + shift
            q, z = jnp.split(u @ b_w_in[l], 2, axis=-1)
            q = rms_norm(q.reshape(bsz, seq, B_HEADS, B_HEAD_DIM), b_q_norm_g[l])
            o = sliding_window_sink_attention(q, k_s, v_s, b_sinks[l], slopes_b)
            o = o.reshape(bsz, seq, B_INNER) * jax.nn.silu(z)
            h = h + gate * (o @ b_w_out[l])
    return h


_drawn_inputs = setup_inputs


def setup_inputs(seed=0):
    import zlib

    import numpy as np

    out = dict(_drawn_inputs(seed))
    spreads = {}
    factors = {'a_norm_g': 8.0,
     'a_ada_b': 3.403,
     'a_q_norm_g': 8.0,
     'a_k_norm_g': 8.0,
     'a_lambda_q1': 4.281,
     'a_lambda_k1': 8.0,
     'a_lambda_q2': 8.0,
     'a_subln_g': 8.0,
     'kv_norm_g': 8.0,
     'kv_ada_b': 8.0,
     'kv_k_norm_g': 8.0,
     'b_norm_g': 8.0,
     'b_ada_b': 7.593,
     'b_q_norm_g': 8.0,
     'b_sinks': 6.439}
    for name, (base, spread) in spreads.items():
        noise = np.random.default_rng([zlib.crc32(name.encode()), seed]).standard_normal(out[name].shape)
        drawn = base * np.exp(spread * noise) if base else spread * noise
        out[name] = __import__('jax').numpy.asarray(drawn.astype(out[name].dtype))
    for name, factor in factors.items():
        out[name] = (out[name] * factor).astype(out[name].dtype)
    return out
```

```python
from contextlib import ExitStack

import numpy as np
import concourse.bass as bass
from concourse import mybir

F32 = mybir.dt.float32
F32R = mybir.dt.float32r
I32 = mybir.dt.int32
ALU = mybir.AluOpType
ACT = mybir.ActivationFunctionType
AX = mybir.AxisListType

P = 128
SEQ = 1024
D = 1024
NT = SEQ // P
KD = D // P
FW = 512
A_HEADS = 8
B_HEADS = 16
B_UNIT = 4
B_UNITS = B_HEADS // B_UNIT
HD = 64
EPS = 1e-6
LAMBDA_INIT = 0.8 - 0.6
MASKED = -1e30
HUGE = 3e38
ADA0 = 2048
ADAW = 768

C_VEC = 0
C_ADAB = C_VEC + KD
C_GA = C_ADAB + 64
C_GKV = C_GA + KD
C_GB = C_GKV + KD
C_AQK = C_GB + KD
C_SUB = C_AQK + 4 * HD
C_KVK = C_SUB + P
C_BQ = C_KVK + 2 * HD
C_SINK = C_BQ + 4 * HD
C_LAM = C_SINK + B_HEADS
N_PAR = C_LAM + 4 * HD

M_A_SHIFT, M_A_SCALE, M_A_GATE, M_KV_SHIFT, M_KV_SCALE, M_B_SHIFT, M_B_SCALE, M_B_GATE = range(0, 64, 8)


def slope_b(head):
    return float(np.float32(2.0 ** (-8.0 * (head + 1) / B_HEADS)))


def at_least(eng, sem, value):
    if not isinstance(value, int) or value > 0:
        eng.wait_ge(sem, value)


def stand_alone(eng, passed):
    eng.sem_inc(passed, 1)


def pipeline(eng, per, blocks, depth, slot):
    for i in range(per):
        slot(0, i, lambda lag, i=i: i >= lag)
    with eng.Fori(1, blocks) as blk:
        for i in range(per):
            slot(blk, i, lambda lag: True)
    for i in range(depth):
        slot(blocks, i, lambda lag, i=i: i < lag)


def score_base(it):
    return {4: 256, 5: 128, 6: 128}.get(it, 0)


def build(nc, x, par, ada0_w, ada1_w, w_a, w_kv, w_b, out):
    h1 = nc.dram_tensor("h1_scratch", [SEQ, D], F32).ap()
    o_a = nc.dram_tensor("oa_scratch", [SEQ, D], F32).ap()
    o_b = nc.dram_tensor("ob_scratch", [SEQ, D], F32).ap()

    ctx = ExitStack()
    with ctx:
        def sb(name, shape, dt=F32):
            return ctx.enter_context(nc.sbuf_tensor(name, shape, dt))

        def sem(name):
            return ctx.enter_context(nc.semaphore(name))

        u_hi = sb("u_hi", [P, KD, SEQ], F32R)
        u_lo = sb("u_lo", [P, KD, SEQ], F32R)
        w_hi = sb("w_hi", [P, KD, FW], F32R)
        w_lo = sb("w_lo", [P, KD, FW], F32R)
        raw = sb("raw", [P, KD, FW])
        kT = sb("kT", [P, 2, 2, SEQ], F32R)
        oT = kT[:, :, :, :].rearrange("p a b n -> p (a b) n")
        vs = sb("vs", [P, NT, 256], F32R)
        qT = sb("qT", [P, 2, 4 * P], F32R)
        p_hi = sb("p_hi", [P, 1024], F32R)
        p_lo = sb("p_lo", [P, 1024], F32R)
        split = sb("split", [P, 4 * 3 * HD], F32R)
        e0 = sb("e0", [P, 2, 1024])
        e1 = sb("e1", [P, 1024])
        stage = sb("stage", [P, 4, FW])
        qn = sb("qn", [P, 256])
        sq = sb("sq", [P, 256])
        bias = sb("bias", [P, 1024])
        ez = sb("ez", [P, 256])
        zs = sb("zs", [P, 8, 256])
        ol = sb("ol", [P, 256])
        ob = sb("ob", [P, 2, 256])
        adabuf = sb("adabuf", [P, 3 * ADAW])
        ada_acc = adabuf[:, 0:ADAW]
        prm = sb("prm", [P, N_PAR])
        ident = sb("ident", [P, P])
        identr = sb("identr", [P, P], F32R)
        ones = sb("ones", [P, 1])
        mod = sb("mod", [P, 64])
        csil = sb("csil", [P, KD])
        cexp = sb("cexp", [P, KD])
        smod = sb("smod", [P, 3, KD])
        var = sb("var", [P, 8])
        y0 = sb("y0", [P, 8])
        ysq = sb("ysq", [P, 8])
        yh = sb("yh", [P, 8])
        rs = sb("rs", [P, 8])
        ssum = sb("ssum", [P, 8])
        oss = sb("oss", [P, 1])
        negm = sb("negm", [P, 2, 4])
        lsum = sb("lsum", [P, 4, 4])
        esnk = sb("esnk", [P, 4])
        nsink = sb("nsink", [P, 4])
        rl = sb("rl", [P, 4, 4])
        l1e = sb("l1e", [P, 2])
        lamt = sb("lamt", [P, 8])
        junk = sb("junk", [P, P])

        def ps(name, shape):
            return ctx.enter_context(nc.psum_tensor(name, shape, F32))

        ps_p = ps("ps_p", [P, 2, 512])
        ps_s = ps("ps_s", [P, 1024])
        ps_t = ps("ps_t", [P, 1024])
        ps_o = ps("ps_o", [P, 2, 512])

        s_par = sem("s_par")
        dve_passed = sem("dve_passed")
        pool_passed = sem("pool_passed")
        s_ident = sem("s_ident")
        s_const = sem("s_const")
        s_cexp = sem("s_cexp")
        s_lam = sem("s_lam")
        ada0_loaded = [sem(f"ada0_loaded{k}") for k in range(2)]
        ada0_used = sem("ada0_used")
        ada0_mm = sem("ada0_mm")
        s_mod = sem("s_mod")
        w_loaded = [sem(f"w_loaded{c}") for c in range(KD)]
        w_hi_done = sem("w_hi_done")
        w_lo_done = sem("w_lo_done")
        w_lo_pool = sem("w_lo_pool")
        w_free = sem("w_free")
        bias_a = sem("bias_a")
        bias_b = sem("bias_b")
        bias_step = sem("bias_step")
        n_x = [sem(f"n_x{k}") for k in range(2)]
        n_ss = sem("n_ss")
        n_var = sem("n_var")
        n_ln = sem("n_ln")
        n_y0 = sem("n_y0")
        n_step = sem("n_step")
        n_norm = sem("n_norm")
        n_tr = sem("n_tr")
        n_umod_d = sem("n_umod_d")
        n_umod_a = sem("n_umod_a")
        n_hi = sem("n_hi")
        u_ready = sem("u_ready")
        k_umod_d = sem("k_umod_d")
        k_umod_a = sem("k_umod_a")
        k_hi = sem("k_hi")
        k_lo = sem("k_lo")
        k_mm = sem("k_mm")
        k_raw = sem("k_raw")
        k_sq = sem("k_sq")
        k_sum = sem("k_sum")
        k_var = sem("k_var")
        k_ln = sem("k_ln")
        k_y0 = sem("k_y0")
        k_step = sem("k_step")
        k_kn = sem("k_kn")
        k_shi = sem("k_shi")
        k_split = sem("k_split")
        k_tr = sem("k_tr")
        k_kT = sem("k_kT")
        k_vhi = sem("k_vhi")
        k_v = sem("k_v")
        c_o = [sem(f"c_o{k}") for k in range(2)]
        c_res = [sem(f"c_res{k}") for k in range(2)]
        c_tr = sem("c_tr")
        c_hi = sem("c_hi")
        c_lo = sem("c_lo")
        c_mm = sem("c_mm")
        c_y = sem("c_y")
        c_sum = sem("c_sum")
        c_st = [sem(f"c_st{k}") for k in range(2)]
        g_cols = sem("g_cols")
        g_mm = sem("g_mm")
        g_tab = sem("g_tab")

        class AttnSems:

            def __init__(self, pre):
                self.proj = sem(pre + "proj")
                self.staged = sem(pre + "staged")
                self.sq = sem(pre + "sq")
                self.ssum = sem(pre + "ssum")
                self.var = sem(pre + "var")
                self.ln = sem(pre + "ln")
                self.y0 = sem(pre + "y0")
                self.step = sem(pre + "step")
                self.rs = sem(pre + "rs")
                self.qn = sem(pre + "qn")
                self.shi = sem(pre + "shi")
                self.split = sem(pre + "split")
                self.tr = sem(pre + "tr")
                self.qkT = sem(pre + "qkT")
                self.s = sem(pre + "s")
                self.m = sem(pre + "m")
                self.e = sem(pre + "e")
                self.ratio = sem(pre + "ratio")
                self.comb = sem(pre + "comb")
                self.pt = sem(pre + "pt")
                self.phi = sem(pre + "phi")
                self.plo = sem(pre + "plo")
                self.pv = sem(pre + "pv")
                self.ol = sem(pre + "ol")
                self.oadd = sem(pre + "oadd")
                self.oss = sem(pre + "oss")
                self.fin = sem(pre + "fin")
                self.st = [sem(f"{pre}st{k}") for k in range(2)]
                self.ez = sem(pre + "ez")
                self.z1 = sem(pre + "z1")
                self.zr = sem(pre + "zr")
                self.zg = sem(pre + "zg")
                self.vhi = sem(pre + "vhi")
                self.v = sem(pre + "v")
                self.tab = sem(pre + "tab")

        a = AttnSems("a_")
        b = AttnSems("b_")
        b_snk = sem("b_snk")
        b_esnk = sem("b_esnk")
        b_nsink = sem("b_nsink")
        ada_loaded = [sem(f"ada_loaded{k}") for k in range(2)]
        ada_scaled = sem("ada_scaled")
        ada_acc_done = sem("ada_acc_done")
        ada_mm = sem("ada_mm")

        block = ctx.enter_context(nc.Block())

        U_OUT_A, U_KV, U_B, U_OUT_B = A_HEADS, A_HEADS + 2, A_HEADS + 3, A_HEADS + 3 + B_UNITS
        POOL_LO = 3
        DVE_LO = KD - POOL_LO

        def low_ready(eng, unit, unit_a, c):
            if c < DVE_LO:
                eng.wait_ge(w_lo_done, 8 * unit + c + 1)
            else:
                eng.wait_ge(w_lo_pool, POOL_LO * unit_a + c - DVE_LO + 1)
        V_KV, V_B = A_HEADS, A_HEADS + 1

        @block.sync
        def _(sp):
            sp.dma_start(prm[:, :], par).then_inc(s_par, 16)
            big = [e0[:, :, :].rearrange("p a n -> p (a n)"), stage[:, :, :].rearrange("p a n -> p (a n)")]
            for c in range(KD):
                at_least(sp, ada0_used, c - 1)
                sp.dma_start(big[c % 2], ada0_w[c]).then_inc(ada0_loaded[c % 2], 16)
            for c in range(KD):
                sp.dma_start(raw[:, c, :], w_a[0, :, c, :]).then_inc(w_loaded[c], 16)

            def norm_loads(src, n0):
                def slot(blk, i, live):
                    n = 4 * blk + i
                    if not live(0):
                        return
                    at_least(sp, n_tr, n + n0 - 1)
                    sp.dma_start(e0[:, i % 2, :], src[bass.ds(n * P, P), :]).then_inc(n_x[i % 2], 16)
                pipeline(sp, 4, NT // 4, 0, slot)

            def attn_io(S, units, w_src, unit0, unit_a0, width, o_dram, with_ada):
                def slot(u, i, live):
                    if not live(0) and 1 <= i <= 4:
                        for c in (2 * i - 2, 2 * i - 1):
                            sp.wait_ge(w_lo_done, 8 * (units + unit0) + c + 1)
                            sp.dma_start(raw[:, c, :], w_src[units + 1, :, c, :]).then_inc(w_loaded[c], 16)
                    if with_ada and live(0):
                        at_least(sp, ada_acc_done, 8 * u + i - 1)
                        sp.dma_start(adabuf[:, ADAW * (1 + i % 2):ADAW * (2 + i % 2)],
                                     ada1_w[u, i, :, :]).then_inc(ada_loaded[i % 2], 16)
                    if live(0) and i >= 2:
                        for c in {2: (0, 1), 3: (2, 3), 4: (4, 5), 5: (6, 7)}.get(i, ()):
                            low_ready(sp, u + unit0, u + unit_a0, c)
                            sp.dma_start(raw[:, c, :], w_src[u + 1, :, c, :]).then_inc(w_loaded[c], 16)
                    if live(6):
                        it = (i - 6) % 8
                        ub = u + (i - 6) // 8
                        sp.wait_ge(S.fin, 8 * u + i - 6 + 1)
                        sp.dma_start(o_dram[it * P:(it + 1) * P, bass.ds(ub * width, width)],
                                     ob[:, it % 2, 0:width]).then_inc(S.st[it % 2], 16)
                pipeline(sp, 8, units, 6, slot)

            def out_io(S, units, res_src, o_dram, dst, n0):
                sp.wait_ge(S.pt, units * NT)

                def slot(blk, i, live):
                    n = 2 * blk + i
                    if live(0):
                        if n0 or not isinstance(blk, int):
                            at_least(sp, c_tr, n + n0 - 1)
                        sp.wait_ge(S.st[i], 16 * (blk + (units - 1) * NT // 2 + 1))
                        sp.dma_start(e0[:, i, :], o_dram[bass.ds(n * P, P), :]).then_inc(c_o[i], 16)
                    if live(1):
                        j = (i - 1) % 2
                        if isinstance(blk, int) and blk == 0:
                            for k in range(2):
                                sp.wait_ge(S.st[k], 16 * units * NT // 2)
                        elif not isinstance(blk, int) or i >= 1 or blk:
                            sp.wait_ge(c_sum, n + n0 - 2)
                        sp.dma_start(stage[:, 2 * j:2 * j + 2, :].rearrange("p a n -> p (a n)"),
                                     res_src[bass.ds((n - 1) * P, P), :]).then_inc(c_res[j], 16)
                    if live(2):
                        j = i % 2
                        sp.wait_ge(c_sum, n + n0 - 1)
                        sp.dma_start(dst[bass.ds((n - 2) * P, P), :],
                                     adabuf[:, j * D:(j + 1) * D]).then_inc(c_st[j], 16)
                pipeline(sp, 2, NT // 2, 2, slot)

            sp.wait_ge(ada0_used, KD)
            norm_loads(x, 0)
            sp.wait_ge(ada0_mm, 1)
            attn_io(a, A_HEADS, w_a, 0, 0, P, o_a, True)
            out_io(a, A_HEADS, x, o_a, h1, 0)
            for c in range(KD):
                sp.wait_ge(w_lo_done, 8 * (U_OUT_A + 1) + c + 1)
                sp.dma_start(raw[:, c, 0:256], w_kv[:, c, :]).then_inc(w_loaded[c], 16)
            for k in range(2):
                sp.wait_ge(c_st[k], 16 * NT // 2)
            norm_loads(h1, NT)
            for c in range(KD):
                sp.wait_ge(w_lo_done, 8 * U_KV + c + 1)
                sp.dma_start(raw[:, c, :], w_b[0, :, c, :]).then_inc(w_loaded[c], 16)
            attn_io(b, B_UNITS, w_b, U_B, A_HEADS, 256, o_b, False)
            out_io(b, B_UNITS, h1, o_b, out, NT)
            for k in range(2):
                sp.wait_ge(c_st[k], 16 * NT)

        @block.gpsimd
        def _(pool):
            pool.memset(ident[:, :], 0.0).then_inc(s_ident, 1)
            pool.wait_ge(s_ident, 1)
            pool.affine_select(out=ident[:, :], in_=ident[:, :], compare_op=ALU.not_equal, fill=1.0, base=0,
                               pattern=[[-1, P]], channel_multiplier=1).then_inc(s_ident, 1)
            pool.wait_ge(s_ident, 2)
            pool.tensor_copy(identr[:, :], ident[:, :]).then_inc(s_ident, 1)
            pool.iota(e1[:, :].bitcast(I32), pattern=[[1, 1024]], base=-896, channel_multiplier=-1).then_inc(bias_step, 1)
            pool.wait_ge(bias_step, 1)
            pool.tensor_copy(bias[:, :], e1[:, :].bitcast(I32)).then_inc(bias_step, 1)
            pool.wait_ge(bias_step, 2)
            pool.tensor_scalar(bias[:, :], bias[:, :], 0.5, 1.0, ALU.mult, ALU.mult).then_inc(bias_step, 1)
            pool.wait_ge(bias_step, 3)
            pool.affine_select(out=bias[:, :], in_=bias[:, :], compare_op=ALU.is_ge, fill=MASKED, base=896,
                               pattern=[[-1, 1024]], channel_multiplier=1).then_inc(bias_a, 1)

            def attn(S, units, u0, unit_a0, zw, is_a):
                zc = FW - zw

                def slot(u, i, live):
                    s = 8 * u + i
                    if live(2):
                        n = s - 2
                        it = (i - 2) % 8
                        st = stage[:, it % 4, :]
                        pool.wait_ge(S.staged, n + 1)
                        pool.wait_ge(S.ez, n + 1)
                        if is_a:
                            pool.tensor_tensor(st[:, zc:FW], st[:, zc:FW], prm[:, C_SUB:C_SUB + P], ALU.mult)
                        stand_alone(pool, pool_passed)
                        pool.tensor_scalar(ez[:, 0:zw], ez[:, 0:zw], 1.0, 1.0, ALU.add, ALU.mult).then_inc(S.z1, 1)
                    if live(0) and i == 1:
                        for c in range(DVE_LO, KD):
                            pool.wait_ge(w_hi_done, 8 * (u + u0) + c + 1)
                            pool.tensor_tensor(w_lo[:, c, :], raw[:, c, :], w_hi[:, c, :].bitcast(F32),
                                               ALU.subtract).then_inc(w_lo_pool, 1)
                    if is_a and live(4):
                        n = s - 4
                        it = (i - 4) % 8
                        st = stage[:, it % 4, :]
                        pool.wait_ge(S.vhi, n + 1)
                        pool.tensor_tensor(vs[:, it, P:256], st[:, 256:384], vs[:, it, 0:P].bitcast(F32),
                                           ALU.subtract).then_inc(S.v, 1)
                    if live(2):
                        n = s - 2
                        st = stage[:, (i - 2) % 4, :]
                        pool.wait_ge(S.zr, n + 1)
                        pool.tensor_tensor(zs[:, (i - 2) % 8, 0:zw], st[:, zc:FW], ez[:, 0:zw], ALU.mult).then_inc(S.zg, 1)
                    if live(0) and is_a:
                        src = adabuf[:, ADAW * (1 + i % 2):ADAW * (2 + i % 2)]
                        pool.wait_ge(ada_loaded[i % 2], 16 * (4 * u + i // 2 + 1))
                        at_least(pool, ada_acc_done, 8 * u + i)
                        if i == 0:
                            at_least(pool, ada_mm, u)
                            stand_alone(pool, pool_passed)
                            pool.tensor_scalar(ada_acc, src, csil[:, 0:1], 1.0, ALU.mult, ALU.mult).then_inc(ada_acc_done, 1)
                        else:
                            stand_alone(pool, pool_passed)
                            pool.tensor_scalar(src, src, csil[:, i:i + 1], 1.0, ALU.mult, ALU.mult).then_inc(ada_scaled, 1)
                            pool.wait_ge(ada_scaled, 7 * u + i)
                            pool.tensor_tensor(ada_acc, ada_acc, src, ALU.add).then_inc(ada_acc_done, 1)
                pipeline(pool, 8, units, 6, slot)

            def out_sums(n0):
                def slot(blk, i, live):
                    if live(1):
                        n = 2 * blk + i - 1 + n0
                        j = (i - 1) % 2
                        yo = adabuf[:, j * D:(j + 1) * D]
                        pool.wait_ge(c_y, 2 * n + 2)
                        pool.wait_ge(c_res[j], 16 * (blk + n0 // 2 + (1 if j == 0 else 0)))
                        pool.tensor_tensor(yo, yo, stage[:, 2 * j:2 * j + 2, :].rearrange("p a n -> p (a n)"),
                                           ALU.add).then_inc(c_sum, 1)
                pipeline(pool, 2, NT // 2, 1, slot)

            pool.wait_ge(s_const, 3)
            pool.wait_ge(s_lam, 4)
            pool.wait_ge(ada0_mm, 1)
            attn(a, A_HEADS, 0, 0, P, True)
            pool.wait_ge(a.m, 2 * A_HEADS * NT)
            pool.wait_ge(a.comb, A_HEADS * NT)
            pool.iota(e1[:, 0:256].bitcast(I32), pattern=[[1, 256]], base=-P, channel_multiplier=-1).then_inc(bias_step, 1)
            pool.wait_ge(bias_step, 4)
            for j, head in enumerate((0, 1, 8, 9)):
                pool.tensor_copy(bias[:, 256 * j:256 * j + 256], e1[:, 0:256].bitcast(I32)).then_inc(bias_step, 1)
            pool.wait_ge(bias_step, 8)
            for j, head in enumerate((0, 1, 8, 9)):
                pool.tensor_scalar(bias[:, 256 * j:256 * j + 256], bias[:, 256 * j:256 * j + 256],
                                   slope_b(head), 1.0, ALU.mult, ALU.mult).then_inc(bias_step, 1)
            pool.wait_ge(bias_step, 12)
            pool.affine_select(out=bias[:, :], in_=bias[:, :], compare_op=ALU.is_ge, fill=MASKED, base=P,
                               pattern=[[0, 4], [-1, 256]], channel_multiplier=1).then_inc(bias_step, 1)
            pool.wait_ge(bias_step, 13)
            pool.affine_select(out=bias[:, :], in_=bias[:, :], compare_op=ALU.is_ge, fill=MASKED, base=-1,
                               pattern=[[0, 4], [1, 256]], channel_multiplier=-1).then_inc(bias_b, 1)
            out_sums(0)

            def kv_slot(blk, i, live):
                if live(3):
                    n = 4 * blk + i - 3
                    pool.wait_ge(k_raw, n + 1)
                    at_n = vs[:, bass.ds(n, 1), :].rearrange("p o (g c) -> p (o g) c", c=P)
                    v_raw = ol[:, P:256].rearrange("p (g c) -> p g c", c=HD)
                    stand_alone(pool, pool_passed)
                    pool.tensor_copy(at_n[:, :, 0:HD], v_raw).then_inc(k_vhi, 1)
                    pool.wait_ge(k_vhi, n + 1)
                    pool.tensor_tensor(at_n[:, :, HD:P], v_raw, at_n[:, :, 0:HD].bitcast(F32),
                                       ALU.subtract).then_inc(k_v, 1)
            pipeline(pool, 4, NT // 4, 3, kv_slot)
            attn(b, B_UNITS, U_B, A_HEADS, 256, False)
            out_sums(NT)

        @block.tensor
        def _(pe):
            def adaln_first():
                pe.wait_ge(s_const, 4)
                pe.wait_ge(ada0_used, KD)
                for j in range(ADA0 // P):
                    mm = pe.matmul(ps_p[:, 0, j:j + 1], adabuf[:, j * P:(j + 1) * P], ones[:, :], start=True, stop=True)
                mm.then_inc(ada0_mm, 1)

            def norm(n0, with_kv):
                def slot(blk, i, live):
                    s = 4 * blk + i
                    if live(1):
                        n = s - 1
                        j = (i - 1) % 2
                        dst = (ps_t, ps_s)[j]
                        pe.wait_ge(n_norm, n + n0 + 1)
                        at_least(pe, n_umod_d, n + n0 - 1)
                        at_least(pe, n_umod_a, n + n0 - 1)
                        if with_kv:
                            at_least(pe, k_umod_d, n - 1)
                            at_least(pe, k_umod_a, n - 1)
                        for d in range(KD):
                            mm = pe.transpose(dst[:, d * P:(d + 1) * P], e0[:, j, d * P:(d + 1) * P], ident[:, :])
                        mm.then_inc(n_tr, 1)
                    if with_kv and live(2):
                        n = s - 2
                        it = (i - 2) % 4
                        last = isinstance(blk, int) and blk == NT // 4 and i == 1
                        pe.wait_ge(k_lo, n + 1)
                        at_least(pe, k_raw, n - 1)
                        for c in range(KD):
                            if isinstance(blk, int) and blk == 0 and i == 2:
                                pe.wait_ge(w_lo_done, 8 * U_KV + c + 1)
                            st_hi, st_lo = p_hi[:, c * P:(c + 1) * P], p_lo[:, c * P:(c + 1) * P]
                            o = ps_o[:, it % 2, 0:256]
                            pe.matmul(o, st_hi, w_hi[:, c, 0:256], start=(c == 0), stop=False)
                            pe.matmul(o, st_hi, w_lo[:, c, 0:256], start=False, stop=False)
                            mm = pe.matmul(o, st_lo, w_hi[:, c, 0:256], start=False, stop=(c == KD - 1))
                            if last and c < KD - 1:
                                mm.then_inc(w_free, 1)
                        mm.then_inc(k_mm, 1)
                        if last:
                            pe.wait_ge(k_mm, NT)
                            pe.nop().then_inc(w_free, 1)
                    if with_kv and live(3):
                        n = s - 3
                        pe.wait_ge(k_split, n + 1)
                        at_least(pe, k_kT, n)
                        for g in range(2):
                            for o in range(2):
                                mm = pe.transpose(ps_p[:, 0, (2 * g + o) * P:(2 * g + o + 1) * P].bitcast(F32R),
                                                  split[:, g * 192 + o * HD:g * 192 + o * HD + P], identr[:, :])
                        mm.then_inc(k_tr, 1)
                pipeline(pe, 4, NT // 4, 3, slot)

            def attn(S, units, v0, u0, u_n0, is_a):
                def project(u, it, n, chunks):
                    o = ps_p[:, it % 2, :]
                    if chunks[0] == 0:
                        at_least(pe, S.staged, n - 1)
                    if isinstance(u, int) and u == 0 and chunks[0] == 0:
                        pe.wait_ge(u_ready, u_n0 + it + 1)
                    for c in chunks:
                        if it == 0:
                            low_ready(pe, u + u0, u + (0 if is_a else A_HEADS), c)
                        t = slice(it * P, (it + 1) * P)
                        pe.matmul(o, u_hi[:, c, t], w_hi[:, c, :], start=(c == 0), stop=False)
                        pe.matmul(o, u_hi[:, c, t], w_lo[:, c, :], start=False, stop=False)
                        mm = pe.matmul(o, u_lo[:, c, t], w_hi[:, c, :], start=False, stop=(c == KD - 1))
                        if it == NT - 1 and c < KD - 1:
                            mm.then_inc(w_free, 1)
                    if chunks[-1] == KD - 1:
                        mm.then_inc(S.proj, 1)
                        if it == NT - 1:
                            pe.wait_ge(S.proj, n + 1)
                            pe.nop().then_inc(w_free, 1)

                def scores_a(sub, it, n):
                    if sub == 0:
                        pe.wait_ge(S.qkT, n + 1)
                    at_least(pe, S.m, 2 * n + sub)
                    base, nk = score_base(it), (it + 1) * P
                    cuts = [0, nk] if nk <= 512 else [0, 512 - base, nk]
                    for lo_k, hi_k in zip(cuts, cuts[1:]):
                        for o in range(2):
                            mm = pe.matmul(ps_s[:, base + lo_k:base + hi_k], qT[:, it % 2, sub * P:(sub + 1) * P],
                                           kT[:, sub, o, lo_k:hi_k], start=(o == 0), stop=(o == 1))
                    mm.then_inc(S.s, 1)

                def scores_b(part, it, n):
                    if part == 0:
                        pe.wait_ge(S.qkT, n + 1)
                    at_least(pe, S.m, 2 * (n - 1) + part + 1)
                    w0 = P if it == 0 else 0
                    for j in (2 * part, 2 * part + 1):
                        for o in range(2):
                            mm = pe.matmul(ps_s[:, j * 256 + w0:j * 256 + 256], qT[:, it % 2, j * P:(j + 1) * P],
                                           kT[:, j // 2, o, (it - 1) * P + w0:(it + 1) * P],
                                           start=(o == 0), stop=(o == 1))
                    mm.then_inc(S.s, 1)

                scores = scores_a if is_a else scores_b

                def slot(u, i, live):
                    s = 8 * u + i
                    n1, n3, n4, n5 = s - 1, s - 3, s - 4, s - 5
                    i1, i3, i4, i5 = (i - 1) % 8, (i - 3) % 8, (i - 4) % 8, (i - 5) % 8
                    u1 = u + (i - 1) // 8
                    if live(4):
                        scores(0, i4, n4)
                    if live(1):
                        project(u1, i1, n1, range(0, 2))
                    if live(4):
                        scores(1, i4, n4)
                    if live(5):
                        pe.wait_ge(S.phi, n5 + 1)
                        pe.wait_ge(S.plo, n5 + 1)
                        if is_a:
                            pe.wait_ge(S.v, n5 + 1)
                            at_least(pe, S.oadd, n5 - 1)
                            o = ps_o[:, i5 % 2, :]
                            if i == 0 and live(8):
                                pe.wait_ge(ada_acc_done, 8 * u)
                                for j in range(ADAW // P):
                                    mm = pe.matmul(o[:, 500 + j:501 + j], ada_acc[:, j * P:(j + 1) * P], ones[:, :],
                                                   start=True, stop=True)
                                mm.then_inc(ada_mm, 1)
                            for j in range(i5 + 1):
                                pe.matmul(o[:, 0:256], p_hi[:, j * P:(j + 1) * P], vs[:, j, :], start=(j == 0), stop=False)
                                mm = pe.matmul(o[:, 0:256], p_lo[:, j * P:(j + 1) * P], vs[:, j, :], start=False,
                                               stop=(j == i5))
                        else:
                            at_least(pe, S.oadd, n5)
                            for j in range(4):
                                o = ps_o[:, j // 2, (j % 2) * 256:(j % 2) * 256 + 256]
                                first = 1 if i5 == 0 else 0
                                for k in range(first, 2):
                                    t = slice((2 * j + k) * P, (2 * j + k + 1) * P)
                                    pe.matmul(o, p_hi[:, t], vs[:, i5 - 1 + k, :], start=(k == first), stop=False)
                                    mm = pe.matmul(o, p_lo[:, t], vs[:, i5 - 1 + k, :], start=False, stop=(k == 1))
                        mm.then_inc(S.pv, 1)
                    if live(3):
                        pe.wait_ge(S.split, n3 + 1)
                        if is_a:
                            for sub in range(2):
                                for o in range(2):
                                    c = (2 + sub) * 192 + o * HD
                                    pe.transpose(ps_t[:, (2 * sub + o) * P:(2 * sub + o + 1) * P].bitcast(F32R),
                                                 split[:, c:c + P], identr[:, :])
                            for sub in range(2):
                                mm = pe.transpose(ps_t[:, 512 + sub * P:512 + (sub + 1) * P].bitcast(F32R),
                                                  split[:, sub * 192:sub * 192 + P], identr[:, :])
                        else:
                            for j in range(4):
                                mm = pe.transpose(ps_t[:, j * P:(j + 1) * P].bitcast(F32R),
                                                  split[:, j * 192:j * 192 + P], identr[:, :])
                        mm.then_inc(S.tr, 1)
                    if live(1):
                        project(u1, i1, n1, range(2, 7))
                    if live(4):
                        pe.wait_ge(S.comb if is_a else S.e, n4 + 1 if is_a else 2 * n4 + 2)
                        if live(3):
                            pe.wait_ge(S.qkT, n3 + 1)
                        if is_a:
                            for j in range(i4 + 1):
                                mm = pe.transpose(ps_t[:, j * P:(j + 1) * P], e0[:, i4 % 2, j * P:(j + 1) * P], ident[:, :])
                        else:
                            for j in range(8):
                                if i4 > 0 or j % 2 == 1:
                                    mm = pe.transpose(ps_t[:, j * P:(j + 1) * P], e0[:, i4 % 2, j * P:(j + 1) * P],
                                                      ident[:, :])
                        mm.then_inc(S.pt, 1)
                    if live(1):
                        project(u1, i1, n1, range(7, KD))
                pipeline(pe, 8, units, 6, slot)

            def gate_rows(k):
                pe.wait_ge(g_cols, k + 1)
                for d in range(KD):
                    mm = pe.matmul(ps_s[:, d * P:(d + 1) * P], adabuf[:, d * P:(d + 1) * P], ident[:, :],
                                   start=True, stop=True)
                mm.then_inc(g_mm, 1)

            def output(n0, u0, k):
                def slot(blk, i, live):
                    if live(0):
                        n = 2 * blk + i + n0
                        pe.wait_ge(c_o[i], 16 * (blk + n0 // 2 + 1))
                        at_least(pe, c_lo, n)
                        for d in range(KD):
                            mm = pe.transpose(ps_t[:, d * P:(d + 1) * P], e0[:, i, d * P:(d + 1) * P], ident[:, :])
                        mm.then_inc(c_tr, 1)
                        if isinstance(blk, int) and blk == 0 and i == 0:
                            gate_rows(k)
                    if live(1):
                        n = 2 * blk + i - 1 + n0
                        j = (i - 1) % 2
                        pe.wait_ge(c_lo, n + 1)
                        at_least(pe, c_y, 2 * (n - 2) + 2)
                        for half in range(2):
                            o = (ps_p, ps_o)[j][:, half, :]
                            for c in range(KD):
                                if isinstance(blk, int) and blk == 0:
                                    pe.wait_ge(w_lo_done, 8 * (u0 + half) + c + 1)
                                hi = oT[:, 2 * j, c * P:(c + 1) * P]
                                lo = oT[:, 2 * j + 1, c * P:(c + 1) * P]
                                f = slice(half * FW, (half + 1) * FW)
                                pe.matmul(o, hi, u_hi[:, c, f], start=(c == 0), stop=False)
                                pe.matmul(o, hi, u_lo[:, c, f], start=False, stop=False)
                                mm = pe.matmul(o, lo, u_hi[:, c, f], start=False, stop=(c == KD - 1))
                            mm.then_inc(c_mm, 1)
                pipeline(pe, 2, NT // 2, 1, slot)

            pe.wait_ge(s_ident, 3)
            adaln_first()
            norm(0, False)
            attn(a, A_HEADS, 0, 0, 0, True)
            output(0, U_OUT_A, 0)
            norm(NT, True)
            pe.wait_ge(k_kT, NT)
            pe.wait_ge(k_v, NT)
            attn(b, B_UNITS, V_B, U_B, NT, False)
            output(NT, U_OUT_B, 1)

        @block.scalar
        def _(act):
            def split_hi(unit, c, dst, free_at, width=FW):
                act.wait_ge(w_loaded[c], 16 * (unit + 1))
                at_least(act, w_free, free_at)
                act.activation(dst, raw[:, c, 0:width], ACT.Copy).then_inc(w_hi_done, 1)

            def norm(n0, with_kv):
                def slot(blk, i, live):
                    s = 4 * blk + i
                    if live(0):
                        n = s
                        act.wait_ge(n_x[i % 2], 16 * (2 * blk + n0 // 2 + i // 2 + 1))
                        at_least(act, n_var, n + n0)
                        at_least(act, n_ss, n + n0)
                        act.activation(stage[:, 0:2, :].rearrange("p a n -> p (a n)"), e0[:, i % 2, :], ACT.Square,
                                       accum_out=ssum[:, 0:1]).then_inc(n_ss, 1)
                    if live(1):
                        n = s - 1
                        src = (ps_t, ps_s)[(i - 1) % 2]
                        act.wait_ge(n_tr, n + n0 + 1)
                        at_least(act, u_ready, n + n0)
                        for d in range(4, KD):
                            last = act.activation(e1[:, d * P:(d + 1) * P], src[:, d * P:(d + 1) * P], ACT.Identity,
                                                  scale=smod[:, 2 if with_kv else 0, d:d + 1],
                                                  bias=mod[:, (M_B_SHIFT if with_kv else M_A_SHIFT) + d:
                                                           (M_B_SHIFT if with_kv else M_A_SHIFT) + d + 1])
                        last.then_inc(n_umod_a, 1)
                        if with_kv:
                            at_least(act, k_lo, n)
                            for d in range(4, KD):
                                last = act.activation(stage[:, 2 + d // 4, (d % 4) * P:(d % 4 + 1) * P],
                                                      src[:, d * P:(d + 1) * P], ACT.Identity,
                                                      scale=smod[:, 1, d:d + 1],
                                                      bias=mod[:, M_KV_SHIFT + d:M_KV_SHIFT + d + 1])
                            last.then_inc(k_umod_a, 1)
                    if live(0):
                        n = s + n0
                        act.wait_ge(n_var, n + 1)
                        act.activation(y0[:, 0:1], var[:, 0:1], ACT.Ln).then_inc(n_ln, 1)
                        act.wait_ge(n_ln, n + 1)
                        act.activation(y0[:, 0:1], y0[:, 0:1], ACT.Exp, scale=-0.5).then_inc(n_y0, 1)
                    if live(1):
                        n = s - 1
                        act.wait_ge(n_umod_d, n + n0 + 1)
                        act.wait_ge(n_umod_a, n + n0 + 1)
                        if n0:
                            if isinstance(blk, int) and blk == 0 and i == 1:
                                act.wait_ge(c_mm, 2 * NT)
                        act.activation(u_hi[:, :, bass.ds(n * P, P)], e1[:, :].rearrange("p (d t) -> p d t", t=P),
                                       ACT.Copy).then_inc(n_hi, 1)
                        if with_kv:
                            act.wait_ge(k_umod_d, n + 1)
                            act.wait_ge(k_umod_a, n + 1)
                            at_least(act, k_mm, n)
                            act.activation(p_hi[:, :], stage[:, 2:4, :].rearrange("p a n -> p (a n)"),
                                           ACT.Copy).then_inc(k_hi, 1)
                    if with_kv and live(3):
                        n = s - 3
                        it = (i - 3) % 4
                        act.wait_ge(k_mm, n + 1)
                        at_least(act, k_v, n)
                        at_least(act, k_kn, n)
                        act.activation(ol[:, :], ps_o[:, it % 2, 0:256], ACT.Copy).then_inc(k_raw, 1)
                        act.wait_ge(k_var, n + 1)
                        act.activation(y0[:, 4:6], var[:, 4:6], ACT.Ln).then_inc(k_ln, 1)
                        act.wait_ge(k_ln, n + 1)
                        act.activation(y0[:, 4:6], y0[:, 4:6], ACT.Exp, scale=-0.5).then_inc(k_y0, 1)
                        act.wait_ge(k_kn, n + 1)
                        at_least(act, k_tr, n)
                        act.activation(split[:, 0:384].rearrange("p (g c) -> p g c", c=192)[:, :, 0:HD],
                                       qn[:, 0:P].rearrange("p (g c) -> p g c", c=HD), ACT.Copy).then_inc(k_shi, 1)
                        act.wait_ge(k_tr, n + 1)
                        act.activation(kT[:, :, :, bass.ds(n * P, P)].rearrange("p a b t -> p (a b) t"),
                                       ps_p[:, 0, :].rearrange("p (g t) -> p g t", t=P), ACT.Copy).then_inc(k_kT, 1)
                pipeline(act, 4, NT // 4, 3, slot)

            def attn(S, units, v0, u0, is_a):
                zw = P if is_a else 256

                def exps(part, it, n):
                    act.wait_ge(S.m, 2 * n + part + 1)
                    ring = it % 4
                    if is_a:
                        e = e0[:, it % 2, 0:(it + 1) * P] if part == 0 else e1[:, 0:(it + 1) * P]
                        act.activation(e, e, ACT.Exp, scale=-1.0, bias=negm[:, it % 2, part:part + 1],
                                       accum_out=lsum[:, ring, part:part + 1]).then_inc(S.e, 1)
                    else:
                        w0 = P if it == 0 else 0
                        for j in (2 * part, 2 * part + 1):
                            e = e0[:, it % 2, j * 256 + w0:j * 256 + 256]
                            last = act.activation(e, e, ACT.Exp, scale=-1.0, bias=negm[:, it % 2, j:j + 1],
                                                  accum_out=lsum[:, ring, j:j + 1])
                        last.then_inc(S.e, 1)

                def slot(u, i, live):
                    s = 8 * u + i
                    n2, n3, n4, n5 = s - 2, s - 3, s - 4, s - 5
                    i2, i3, i4, i5 = (i - 2) % 8, (i - 3) % 8, (i - 4) % 8, (i - 5) % 8

                    def split_next(chunks):
                        for c in chunks:
                            split_hi(u + u0, c, w_hi[:, c, :], 8 * (u + v0 - 1) + c + 1)
                    if live(2):
                        act.wait_ge(S.proj, n2 + 1)
                        at_least(act, S.ssum, n2)
                        act.activation(sq[:, :], ps_p[:, i2 % 2, 0:256], ACT.Square).then_inc(S.sq, 1)
                        at_least(act, S.zg, n2)
                        if is_a:
                            at_least(act, S.v, n2 - 3)
                        act.activation(stage[:, i2 % 4, :], ps_p[:, i2 % 2, :], ACT.Copy).then_inc(S.staged, 1)
                        act.wait_ge(S.staged, n2 + 1)
                        act.activation(ez[:, 0:zw], stage[:, i2 % 4, FW - zw:FW], ACT.Exp, scale=-1.0).then_inc(S.ez, 1)
                    if live(0) and i == 1:
                        split_next((4,))
                    if live(4):
                        exps(0, i4, n4)
                    if not (isinstance(u, int) and u == 0 and i < 2) and (is_a or live(2)):
                        act.wait_ge(S.var, s - 1)
                        act.activation(y0[:, 0:5], var[:, 0:5], ACT.Ln).then_inc(S.ln, 1)
                        act.wait_ge(S.ln, s - 1)
                        act.activation(y0[:, 0:5], y0[:, 0:5], ACT.Exp, scale=-0.5).then_inc(S.y0, 1)
                    if live(0) and i == 1:
                        split_next((5, 6, 7))
                    if live(4):
                        exps(1, i4, n4)
                        if not is_a:
                            act.wait_ge(b_snk, n4 + 1)
                            act.activation(esnk[:, :], esnk[:, :], ACT.Exp).then_inc(b_esnk, 1)
                    if live(3):
                        act.wait_ge(S.tr, n3 + 1)
                        if is_a:
                            act.activation(kT[:, :, :, i3 * P:(i3 + 1) * P].rearrange("p a b t -> p (a b) t"),
                                           ps_t[:, 0:512].rearrange("p (g t) -> p g t", t=P), ACT.Copy)
                            act.activation(qT[:, i3 % 2, 0:256], ps_t[:, 512:768], ACT.Copy).then_inc(S.qkT, 1)
                        else:
                            act.activation(qT[:, i3 % 2, :], ps_t[:, 0:512], ACT.Copy).then_inc(S.qkT, 1)
                    if live(5):
                        act.wait_ge(S.pv, n5 + 1)
                        at_least(act, S.oadd, n5)
                        if is_a:
                            act.activation(ol[:, 0:P], ps_o[:, i5 % 2, P:256], ACT.Copy).then_inc(S.ol, 1)
                        else:
                            for g in range(2):
                                src = ps_o[:, g, :].rearrange("p (j c) -> p j c", c=256)[:, :, g * P + HD:g * P + P]
                                last = act.activation(ol[:, g * P:(g + 1) * P].rearrange("p (j c) -> p j c", c=HD),
                                                      src, ACT.Copy)
                            last.then_inc(S.ol, 1)
                    if live(2):
                        act.wait_ge(S.qn, n2 + 1)
                        at_least(act, S.tr, n2)
                        act.activation(split[:, :].rearrange("p (g c) -> p g c", c=192)[:, :, 0:HD],
                                       qn[:, :].rearrange("p (g c) -> p g c", c=HD), ACT.Copy).then_inc(S.shi, 1)
                    if is_a and live(4):
                        if i4 == 0:
                            at_least(act, S.pv, n4)
                        act.activation(vs[:, i4, 0:P], stage[:, i4 % 4, 256:384], ACT.Copy).then_inc(S.vhi, 1)
                    if live(0) and i == 0:
                        split_next((0, 1))
                    if live(4):
                        act.wait_ge(S.pt, n4 + 1)
                        if is_a:
                            nk = (i4 + 1) * P
                            for c0 in range(0, nk, 512):
                                c1 = min(c0 + 512, nk)
                                last = act.activation(p_hi[:, c0:c1], ps_t[:, c0:c1], ACT.Copy)
                        else:
                            for g in range(2):
                                w0 = P if i4 == 0 else 0
                                o, src = (v[:, g * 512:(g + 1) * 512].rearrange("p (j c) -> p j c", c=256)[:, :, w0:256]
                                          for v in (p_hi, ps_t))
                                last = act.activation(o, src, ACT.Copy)
                        last.then_inc(S.phi, 1)
                    if live(0) and i == 0:
                        split_next((2, 3))
                    if not live(0) and i < 4:
                        for c in (2 * i, 2 * i + 1):
                            split_hi(units + u0, c, u_hi[:, c, 0:FW], 8 * (units + v0))
                pipeline(act, 8, units, 6, slot)

            def output(n0, u0, free_at):
                def slot(blk, i, live):
                    if live(0):
                        n = 2 * blk + i + n0
                        act.wait_ge(c_tr, n + 1)
                        at_least(act, c_mm, 2 * (n - 2) + 2)
                        for g in range(2):
                            last = act.activation(oT[:, 2 * i, g * 512:(g + 1) * 512], ps_t[:, g * 512:(g + 1) * 512],
                                                  ACT.Copy)
                        last.then_inc(c_hi, 1)
                        if isinstance(blk, int) and blk == 0 and i == 0:
                            for c in range(KD):
                                split_hi(u0 + 1, c, u_hi[:, c, FW:2 * FW], free_at)
                pipeline(act, 2, NT // 2, 1, slot)

            nc.scalar.preload_act_table_set("natural_log_exp_and_others")
            act.wait_ge(s_par, 16)
            act.activation(cexp[:, :], prm[:, C_VEC:C_VEC + KD], ACT.Exp, scale=-1.0).then_inc(s_cexp, 1)
            act.wait_ge(s_lam, 2)
            act.activation(lamt[:, 2:4], lamt[:, 0:2], ACT.Exp).then_inc(s_cexp, 1)
            act.wait_ge(s_mod, 3)
            act.wait_ge(bias_a, 1)
            norm(0, False)
            attn(a, A_HEADS, 0, 0, True)
            output(0, U_OUT_A, 8 * A_HEADS)
            for c in range(KD):
                split_hi(U_KV, c, w_hi[:, c, 0:256], 8 * V_KV, 256)
            act.wait_ge(s_mod, 5 + A_HEADS)
            norm(NT, True)
            attn(b, B_UNITS, V_B, U_B, False)
            output(NT, U_OUT_B, 8 * (V_B + B_UNITS))

        @block.vector
        def _(dve):
            def split_lo(unit, c, dst, hi, width=FW, step=1):
                dve.wait_ge(w_hi_done, 8 * unit + c + 1)
                dve.tensor_tensor(dst, raw[:, c, 0:width], hi.bitcast(F32), ALU.subtract).then_inc(w_lo_done, step)

            def newton(v, y, w, sem_y0, y0_at, step, step_at, out_rs, sem_rs):
                dve.wait_ge(sem_y0, y0_at)
                dve.tensor_tensor(ysq[:, w], y, y, ALU.mult).then_inc(step, 1)
                dve.wait_ge(step, step_at + 1)
                dve.scalar_tensor_tensor(out=yh[:, w], in0=ysq[:, w], scalar=-0.5, in1=v, op0=ALU.mult,
                                         op1=ALU.mult).then_inc(step, 1)
                dve.wait_ge(step, step_at + 2)
                dve.scalar_tensor_tensor(out=out_rs, in0=yh[:, w], scalar=1.5, in1=y, op0=ALU.add,
                                         op1=ALU.mult).then_inc(sem_rs, 1)

            def modulate(src, dst, k, shift, last_sem):
                for d in range(4):
                    last = dve.tensor_scalar(dst(d), src[:, d * P:(d + 1) * P], smod[:, k, d:d + 1],
                                             mod[:, shift + d:shift + d + 1], ALU.mult, ALU.add)
                last.then_inc(last_sem, 1)

            def norm(n0, with_kv):
                def slot(blk, i, live):
                    s = 4 * blk + i
                    if live(0):
                        n = s + n0
                        dve.wait_ge(n_ss, n + 1)
                        dve.tensor_scalar(var[:, 0:1], ssum[:, 0:1], 1.0 / D, EPS, ALU.mult, ALU.add).then_inc(n_var, 1)
                    if live(1):
                        n = s - 1
                        src = (ps_t, ps_s)[(i - 1) % 2]
                        dve.wait_ge(n_tr, n + n0 + 1)
                        at_least(dve, u_ready, n + n0)
                        modulate(src, lambda d: e1[:, d * P:(d + 1) * P], 2 if with_kv else 0,
                                 M_B_SHIFT if with_kv else M_A_SHIFT, n_umod_d)
                        if with_kv:
                            at_least(dve, k_lo, n)
                            modulate(src, lambda d: stage[:, 2, d * P:(d + 1) * P], 1, M_KV_SHIFT, k_umod_d)
                    if live(0):
                        n = s + n0
                        at_least(dve, n_norm, n)
                        newton(var[:, 0:1], y0[:, 0:1], slice(0, 1), n_y0, n + 1, n_step, 3 * n, rs[:, 0:1], n_step)
                        dve.wait_ge(n_step, 3 * n + 3)
                        dve.tensor_scalar(e0[:, i % 2, :], e0[:, i % 2, :], rs[:, 0:1], None,
                                          ALU.mult).then_inc(n_norm, 1)
                    if live(1):
                        n = s - 1
                        dve.wait_ge(n_hi, n + n0 + 1)
                        dve.tensor_tensor(u_lo[:, :, bass.ds(n * P, P)], e1[:, :].rearrange("p (d t) -> p d t", t=P),
                                          u_hi[:, :, bass.ds(n * P, P)].bitcast(F32), ALU.subtract).then_inc(u_ready, 1)
                        if with_kv:
                            dve.wait_ge(k_hi, n + 1)
                            dve.tensor_tensor(p_lo[:, :], stage[:, 2:4, :].rearrange("p a n -> p (a n)"),
                                              p_hi[:, :].bitcast(F32), ALU.subtract).then_inc(k_lo, 1)
                    if with_kv and live(3):
                        n = s - 3
                        dve.wait_ge(k_raw, n + 1)
                        at_least(dve, k_split, n)
                        dve.tensor_tensor(sq[:, 0:P], ol[:, 0:P], ol[:, 0:P], ALU.mult).then_inc(k_sq, 1)
                        dve.wait_ge(k_sq, n + 1)
                        dve.tensor_reduce(ssum[:, 4:6], sq[:, 0:P].rearrange("p (g c) -> p g c", c=HD), AX.X,
                                          ALU.add).then_inc(k_sum, 1)
                        dve.wait_ge(k_sum, n + 1)
                        dve.tensor_scalar(var[:, 4:6], ssum[:, 4:6], 1.0 / HD, EPS, ALU.mult, ALU.add).then_inc(k_var, 1)
                        newton(var[:, 4:6], y0[:, 4:6], slice(4, 6), k_y0, n + 1, k_step, 3 * n, rs[:, 4:6], k_step)
                        dve.wait_ge(k_step, 3 * n + 3)
                        for g in range(2):
                            last = dve.scalar_tensor_tensor(out=qn[:, g * HD:(g + 1) * HD], in0=ol[:, g * HD:(g + 1) * HD],
                                                            scalar=rs[:, 4 + g:5 + g],
                                                            in1=prm[:, C_KVK + g * HD:C_KVK + (g + 1) * HD],
                                                            op0=ALU.mult, op1=ALU.mult)
                        last.then_inc(k_kn, 1)
                        dve.wait_ge(k_shi, n + 1)
                        sp3 = split[:, 0:384].rearrange("p (g c) -> p g c", c=192)
                        dve.tensor_copy(sp3[:, :, 2 * HD:3 * HD], sp3[:, :, 0:HD].bitcast(F32))
                        dve.tensor_tensor(sp3[:, :, HD:2 * HD], qn[:, 0:P].rearrange("p (g c) -> p g c", c=HD),
                                          sp3[:, :, 0:HD].bitcast(F32), ALU.subtract).then_inc(k_split, 1)
                pipeline(dve, 4, NT // 4, 3, slot)

            def attn(S, units, u0, is_a):
                zw = P if is_a else 256

                def masked_max(part, it, n):
                    at_least(dve, S.pt, n - 1)
                    dve.wait_ge(S.s, 2 * n + part + 1)
                    stand_alone(dve, dve_passed)
                    if is_a:
                        nk = (it + 1) * P
                        base = score_base(it)
                        e = e0[:, it % 2, 0:nk] if part == 0 else e1[:, 0:nk]
                        dve.tensor_tensor_reduce(e, ps_s[:, base:base + nk], bias[:, 1024 - nk:1024], -1.0, HUGE,
                                                 ALU.add, ALU.min, negm[:, it % 2, part:part + 1]).then_inc(S.m, 1)
                    else:
                        w0 = P if it == 0 else 0
                        for j in (2 * part, 2 * part + 1):
                            t = slice(j * 256 + w0, j * 256 + 256)
                            last = dve.tensor_tensor_reduce(e0[:, it % 2, t], ps_s[:, t], bias[:, t], -1.0,
                                                            nsink[:, j:j + 1], ALU.add, ALU.min,
                                                            negm[:, it % 2, j:j + 1])
                        last.then_inc(S.m, 1)

                def slot(u, i, live):
                    s = 8 * u + i
                    n2, n3, n4, n5, n6 = s - 2, s - 3, s - 4, s - 5, s - 6
                    i2, i4, i5, i6 = (i - 2) % 8, (i - 4) % 8, (i - 5) % 8, (i - 6) % 8
                    first = isinstance(u, int) and u == 0
                    stats = not (first and i < 2) and (is_a or live(2))

                    def split_next(chunks):
                        for c in chunks:
                            split_lo(u + u0, c, w_lo[:, c, :], w_hi[:, c, :], step=8 - c if c == DVE_LO - 1 else 1)

                    def normalise():
                        if stats:
                            if live(3):
                                at_least(dve, S.qn, n2)
                            if is_a:
                                at_least(dve, S.fin, n6)
                            newton(var[:, 0:5], y0[:, 0:5], slice(0, 5), S.y0, s - 1, S.step, 2 * (s - 2), rs[:, 0:5], S.rs)
                        if live(2):
                            dve.wait_ge(S.rs, s - 1)
                            dve.wait_ge(S.staged, n2 + 1)
                            at_least(dve, S.split, n2)
                            g0 = C_AQK if is_a else C_BQ
                            for g in range(4):
                                t = slice(g * HD, (g + 1) * HD)
                                last = dve.scalar_tensor_tensor(out=qn[:, t], in0=stage[:, i2 % 4, t],
                                                                scalar=rs[:, g:g + 1],
                                                                in1=prm[:, g0 + g * HD:g0 + (g + 1) * HD],
                                                                op0=ALU.mult, op1=ALU.mult)
                            last.then_inc(S.qn, 1)

                    if live(4) and i == 4 and not first:
                        at_least(dve, S.m, 2 * n4)
                        dve.tensor_scalar(bias[:, :], bias[:, :], 0.5, None, ALU.mult).then_inc(S.tab, 1)
                        if not is_a:
                            dve.wait_ge(b_snk, n4)
                            dve.tensor_scalar(nsink[:, :], prm[:, bass.ds(4 * u + C_SINK, 4)], -1.0, None,
                                              ALU.mult).then_inc(b_nsink, 1)
                            dve.wait_ge(b_nsink, u + 1)
                        dve.wait_ge(S.tab, u)
                    if live(4):
                        masked_max(0, i4, n4)
                    if live(2):
                        dve.wait_ge(S.sq, n2 + 1)
                        at_least(dve, S.var, s - 2)
                        dve.tensor_reduce(ssum[:, 0:4], sq[:, :].rearrange("p (g c) -> p g c", c=HD), AX.X,
                                          ALU.add).then_inc(S.ssum, 1)
                    if stats:
                        at_least(dve, S.rs, s - 2)
                        if live(6) and is_a:
                            dve.wait_ge(S.oss, n6 + 1)
                            dve.wait_ge(S.ratio, 3 * n6 + 2)
                            last = dve.scalar_tensor_tensor(out=var[:, 4:5], in0=oss[:, :], scalar=1.0 / P,
                                                            in1=l1e[:, i6 % 2:i6 % 2 + 1], op0=ALU.mult, op1=ALU.add)
                        if live(2):
                            dve.wait_ge(S.ssum, n2 + 1)
                            last = dve.tensor_scalar(var[:, 0:4], ssum[:, 0:4], 1.0 / HD, EPS, ALU.mult, ALU.add)
                        if not live(2) and not (live(6) and is_a):
                            last = dve.tensor_copy(junk[:, 0:1], ones[:, :])
                        last.then_inc(S.var, 1)
                    if live(0) and i == 1:
                        split_next((4,))
                    if i4 >= 4:
                        normalise()
                    if live(4):
                        if is_a:
                            at_least(dve, S.comb, n4)
                        masked_max(1, i4, n4)
                        if not is_a:
                            at_least(dve, S.ratio, 2 * n4)
                            dve.wait_ge(S.m, 2 * n4 + 2)
                            dve.tensor_tensor(esnk[:, :], negm[:, i4 % 2, :], nsink[:, :], ALU.subtract).then_inc(b_snk, 1)
                    if i4 < 4:
                        normalise()
                    if live(4) and is_a:
                        dve.wait_ge(S.e, 2 * n4 + 2)
                        at_least(dve, S.ratio, 3 * n4)
                        at_least(dve, S.comb, n4)
                        if live(6):
                            at_least(dve, S.var, s - 1)
                        l = lsum[:, i4 % 4, :]
                        dve.reciprocal(rl[:, 0, 0:1], l[:, 1:2]).then_inc(S.ratio, 1)
                        dve.scalar_tensor_tensor(out=l1e[:, i4 % 2:i4 % 2 + 1], in0=l[:, 0:1], scalar=EPS, in1=l[:, 0:1],
                                                 op0=ALU.mult, op1=ALU.mult).then_inc(S.ratio, 1)
                        dve.wait_ge(S.ratio, 3 * n4 + 1)
                        dve.scalar_tensor_tensor(out=rl[:, 1, 0:1], in0=rl[:, 0, 0:1], scalar=lamt[:, 6:7],
                                                 in1=l[:, 0:1], op0=ALU.mult, op1=ALU.mult).then_inc(S.ratio, 1)
                        dve.wait_ge(S.ratio, 3 * n4 + 3)
                        nk = (i4 + 1) * P
                        dve.scalar_tensor_tensor(out=e0[:, i4 % 2, 0:nk], in0=e1[:, 0:nk], scalar=rl[:, 1, 0:1],
                                                 in1=e0[:, i4 % 2, 0:nk], op0=ALU.mult, op1=ALU.add).then_inc(S.comb, 1)
                    if live(4) and not is_a:
                        dve.wait_ge(b_esnk, n4 + 1)
                        dve.wait_ge(S.e, 2 * n4 + 2)
                        dve.tensor_tensor(lsum[:, i4 % 4, :], lsum[:, i4 % 4, :], esnk[:, :], ALU.add).then_inc(S.ratio, 1)
                        dve.wait_ge(S.ratio, 2 * n4 + 1)
                        dve.reciprocal(rl[:, i4 % 4, :], lsum[:, i4 % 4, :]).then_inc(S.ratio, 1)
                    if live(5):
                        dve.wait_ge(S.ol, n5 + 1)
                        at_least(dve, S.st[i5 % 2], 16 * (4 * (u + (i - 5) // 8) + i5 // 2))
                        if is_a:
                            dve.tensor_tensor(ob[:, i5 % 2, 0:P], ps_o[:, i5 % 2, 0:P], ol[:, 0:P],
                                              ALU.add).then_inc(S.oadd, 1)
                            if i == 0 and live(8):
                                dve.wait_ge(ada_mm, u)
                                c0 = ADA0 // P + (ADAW // P) * (u - 1)
                                dve.tensor_tensor(mod[:, bass.ds(c0, ADAW // P)], ps_o[:, i5 % 2, 500:500 + ADAW // P],
                                                  prm[:, bass.ds(c0 + C_ADAB, ADAW // P)], ALU.add).then_inc(s_mod, 1)
                            dve.wait_ge(S.oadd, n5 + 1)
                            at_least(dve, S.var, s - 1)
                            stand_alone(dve, dve_passed)
                            dve.tensor_tensor_reduce(junk[:, :], ob[:, i5 % 2, 0:P], ob[:, i5 % 2, 0:P], 1.0, 0.0,
                                                     ALU.mult, ALU.add, oss[:, :]).then_inc(S.oss, 1)
                        else:
                            for g in range(2):
                                src = ps_o[:, g, :].rearrange("p (j c) -> p j c", c=256)[:, :, g * P:g * P + HD]
                                t = slice(g * P, (g + 1) * P)
                                last = dve.tensor_tensor(ob[:, i5 % 2, t].rearrange("p (j c) -> p j c", c=HD), src,
                                                         ol[:, t].rearrange("p (j c) -> p j c", c=HD), ALU.add)
                            last.then_inc(S.oadd, 1)
                    if live(2):
                        dve.wait_ge(S.shi, n2 + 1)
                        sp3 = split[:, :].rearrange("p (g c) -> p g c", c=192)
                        if is_a:
                            dve.tensor_copy(sp3[:, 2:4, 2 * HD:3 * HD], sp3[:, 2:4, 0:HD].bitcast(F32))
                        dve.tensor_tensor(sp3[:, :, HD:2 * HD], qn[:, :].rearrange("p (g c) -> p g c", c=HD),
                                          sp3[:, :, 0:HD].bitcast(F32), ALU.subtract).then_inc(S.split, 1)
                    if live(6):
                        dve.wait_ge(S.zg, n6 + 1)
                        o, z = ob[:, i6 % 2, :], zs[:, i6, :]
                        if is_a:
                            dve.wait_ge(S.rs, s - 1)
                            dve.scalar_tensor_tensor(out=o[:, 0:P], in0=o[:, 0:P], scalar=rs[:, 4:5], in1=z[:, 0:P],
                                                     op0=ALU.mult, op1=ALU.mult).then_inc(S.fin, 1)
                        else:
                            dve.wait_ge(S.oadd, n6 + 1)
                            dve.wait_ge(S.ratio, 2 * n6 + 2)
                            for j in range(4):
                                t = slice(j * HD, (j + 1) * HD)
                                last = dve.scalar_tensor_tensor(out=o[:, t], in0=o[:, t], scalar=rl[:, i6 % 4, j:j + 1],
                                                                in1=z[:, t], op0=ALU.mult, op1=ALU.mult)
                            last.then_inc(S.fin, 1)
                    if live(2):
                        dve.wait_ge(S.z1, n2 + 1)
                        dve.reciprocal(ez[:, 0:zw], ez[:, 0:zw]).then_inc(S.zr, 1)
                    if live(0) and i == 0:
                        split_next((0, 1))
                    if live(4):
                        dve.wait_ge(S.phi, n4 + 1)
                        if is_a:
                            nk = (i4 + 1) * P
                            for c0 in range(0, nk, 512):
                                c1 = min(c0 + 512, nk)
                                last = dve.tensor_tensor(p_lo[:, c0:c1], ps_t[:, c0:c1], p_hi[:, c0:c1].bitcast(F32),
                                                         ALU.subtract)
                        else:
                            w0 = P if i4 == 0 else 0
                            for g in range(2):
                                o, src, hi = (v[:, g * 512:(g + 1) * 512].rearrange("p (j c) -> p j c", c=256)[:, :, w0:256]
                                              for v in (p_lo, ps_t, p_hi))
                                last = dve.tensor_tensor(o, src, hi.bitcast(F32), ALU.subtract)
                        last.then_inc(S.plo, 1)
                    if live(0) and i == 0:
                        split_next((2, 3))
                    if not live(0) and i < 4:
                        for c in (2 * i, 2 * i + 1):
                            split_lo(units + u0, c, u_lo[:, c, 0:FW], u_hi[:, c, 0:FW])
                pipeline(dve, 8, units, 6, slot)

            def gate_columns(col, y_done):
                at_least(dve, c_sum, y_done)
                at_least(dve, c_st[0], 8 * y_done)
                at_least(dve, c_st[1], 8 * y_done)
                dve.tensor_copy(adabuf[:, 0:D].rearrange("p (d t) -> p d t", t=P),
                                mod[:, col:col + KD].unsqueeze(2).to_broadcast([P, KD, P])).then_inc(g_cols, 1)

            def gate_table(k):
                dve.wait_ge(g_mm, k + 1)
                for g in range(2):
                    last = dve.tensor_copy(e1[:, g * 512:(g + 1) * 512], ps_s[:, g * 512:(g + 1) * 512])
                last.then_inc(g_tab, 1)

            def output(n0, u0, k):
                def slot(blk, i, live):
                    if live(0):
                        n = 2 * blk + i + n0
                        dve.wait_ge(c_hi, n + 1)
                        for g in range(2):
                            t = slice(g * 512, (g + 1) * 512)
                            last = dve.tensor_tensor(oT[:, 2 * i + 1, t], ps_t[:, t], oT[:, 2 * i, t].bitcast(F32),
                                                     ALU.subtract)
                        last.then_inc(c_lo, 1)
                        if isinstance(blk, int) and blk == 0 and i == 0:
                            gate_table(k)
                            for c in range(KD):
                                split_lo(u0 + 1, c, u_lo[:, c, FW:2 * FW], u_hi[:, c, FW:2 * FW])
                    if live(1):
                        n = 2 * blk + i - 1 + n0
                        j = (i - 1) % 2
                        if isinstance(blk, int) and blk == 0:
                            dve.wait_ge(g_tab, k + 1)
                        if n0 or not (isinstance(blk, int) and blk == 0):
                            at_least(dve, c_st[j], 16 * (blk + n0 // 2 - (0 if j == 0 else 1)))
                        for half in range(2):
                            dve.wait_ge(c_mm, 2 * n + half + 1)
                            t = slice(half * FW, (half + 1) * FW)
                            dve.tensor_tensor(adabuf[:, j * D + half * FW:j * D + (half + 1) * FW],
                                              (ps_p, ps_o)[j][:, half, :], e1[:, t], ALU.mult).then_inc(c_y, 1)
                pipeline(dve, 2, NT // 2, 1, slot)

            dve.memset(ones[:, :], 1.0)
            dve.memset(var[:, :], 1.0).then_inc(s_const, 1)
            dve.wait_ge(s_par, 16)
            dve.wait_ge(s_cexp, 1)
            dve.tensor_scalar(cexp[:, :], cexp[:, :], 1.0, None, ALU.add).then_inc(s_lam, 1)
            dve.tensor_scalar(prm[:, C_AQK:C_AQK + 2 * HD], prm[:, C_AQK:C_AQK + 2 * HD], HD ** -0.5, None, ALU.mult)
            dve.tensor_scalar(prm[:, C_BQ:C_BQ + 4 * HD], prm[:, C_BQ:C_BQ + 4 * HD], HD ** -0.5, None,
                              ALU.mult).then_inc(s_const, 1)
            dve.tensor_scalar(prm[:, C_SUB:C_SUB + P], prm[:, C_SUB:C_SUB + P], 1.0 - LAMBDA_INIT, None,
                              ALU.mult).then_inc(s_const, 1)
            dve.tensor_scalar(nsink[:, :], prm[:, C_SINK:C_SINK + 4], -1.0, None, ALU.mult).then_inc(b_nsink, 1)
            for k in range(2):
                c = C_LAM + 2 * k * HD
                last = dve.tensor_tensor_reduce(junk[:, k * HD:(k + 1) * HD], prm[:, c:c + HD], prm[:, c + HD:c + 2 * HD],
                                                1.0, 0.0, ALU.mult, ALU.add, lamt[:, k:k + 1])
            last.then_inc(s_lam, 1)
            dve.wait_ge(s_lam, 2)
            dve.reciprocal(csil[:, :], cexp[:, :]).then_inc(s_lam, 1)
            dve.wait_ge(s_lam, 3)
            dve.tensor_tensor(csil[:, :], csil[:, :], prm[:, C_VEC:C_VEC + KD], ALU.mult).then_inc(s_lam, 1)
            dve.wait_ge(s_cexp, 2)
            dve.tensor_tensor(lamt[:, 4:5], lamt[:, 2:3], lamt[:, 3:4], ALU.subtract).then_inc(s_lam, 1)
            dve.wait_ge(s_lam, 5)
            dve.tensor_scalar(lamt[:, 6:7], lamt[:, 4:5], LAMBDA_INIT, -1.0, ALU.add, ALU.mult).then_inc(s_lam, 1)
            dve.wait_ge(s_lam, 6)

            big = [e0[:, :, :].rearrange("p a n -> p (a n)"), stage[:, :, :].rearrange("p a n -> p (a n)")]
            for c in range(KD):
                dve.wait_ge(ada0_loaded[c % 2], 16 * (c // 2 + 1))
                if c == 0:
                    dve.tensor_scalar(adabuf[:, 0:ADA0], big[0], csil[:, 0:1], None, ALU.mult).then_inc(ada0_used, 1)
                else:
                    dve.wait_ge(ada0_used, c)
                    dve.scalar_tensor_tensor(out=adabuf[:, 0:ADA0], in0=big[c % 2], scalar=csil[:, c:c + 1],
                                             in1=adabuf[:, 0:ADA0], op0=ALU.mult, op1=ALU.add).then_inc(ada0_used, 1)
            dve.memset(junk[:, 0:1], 0.0).then_inc(s_const, 1)
            dve.wait_ge(ada0_mm, 1)
            dve.tensor_tensor(mod[:, 0:ADA0 // P], ps_p[:, 0, 0:ADA0 // P], prm[:, C_ADAB:C_ADAB + ADA0 // P],
                              ALU.add).then_inc(s_mod, 1)
            dve.wait_ge(s_mod, 1)
            dve.scalar_tensor_tensor(out=smod[:, 0, :], in0=mod[:, M_A_SCALE:M_A_SCALE + KD], scalar=1.0,
                                     in1=prm[:, C_GA:C_GA + KD], op0=ALU.add, op1=ALU.mult).then_inc(s_mod, 2)
            dve.wait_ge(s_mod, 3)
            dve.wait_ge(bias_a, 1)
            norm(0, False)
            attn(a, A_HEADS, 0, True)
            dve.wait_ge(s_mod, 3 + A_HEADS)
            dve.scalar_tensor_tensor(out=smod[:, 1, :], in0=mod[:, M_KV_SCALE:M_KV_SCALE + KD], scalar=1.0,
                                     in1=prm[:, C_GKV:C_GKV + KD], op0=ALU.add, op1=ALU.mult).then_inc(s_mod, 1)
            dve.scalar_tensor_tensor(out=smod[:, 2, :], in0=mod[:, M_B_SCALE:M_B_SCALE + KD], scalar=1.0,
                                     in1=prm[:, C_GB:C_GB + KD], op0=ALU.add, op1=ALU.mult).then_inc(s_mod, 1)
            dve.wait_ge(bias_step, 12)
            gate_columns(M_A_GATE, 0)
            output(0, U_OUT_A, 0)
            for c in range(KD):
                split_lo(U_KV, c, w_lo[:, c, 0:256], w_hi[:, c, 0:256], 256)
            dve.wait_ge(s_mod, 5 + A_HEADS)
            norm(NT, True)
            dve.wait_ge(bias_b, 1)
            attn(b, B_UNITS, U_B, False)
            gate_columns(M_B_GATE, NT)
            output(NT, U_OUT_B, 1)


def kernel(**inputs):
    import concourse.bacc as bacc
    from concourse.bass_utils import run_bass_kernel_spmd

    f = {k: np.asarray(v) for k, v in inputs.items()}
    col = lambda v: v.reshape(-1, P).T
    row = lambda v: np.broadcast_to(v.reshape(1, -1), (P, v.size))
    units = lambda w: w.reshape(KD, P, -1, FW).transpose(2, 1, 0, 3)

    ada_b = np.concatenate([f["a_ada_b"][0], f["kv_ada_b"], f["b_ada_b"][0]])
    heads = np.arange(B_HEADS).reshape(2, B_UNITS, 2).transpose(1, 0, 2).reshape(-1)
    par = np.concatenate([
        col(f["c"][0]), col(ada_b), col(f["a_norm_g"][0]), col(f["kv_norm_g"]), col(f["b_norm_g"][0]),
        row(f["a_q_norm_g"][0]), row(f["a_q_norm_g"][0]), row(f["a_k_norm_g"][0]), row(f["a_k_norm_g"][0]),
        row(f["a_subln_g"][0]), row(f["kv_k_norm_g"]), row(f["kv_k_norm_g"]),
        *[row(f["b_q_norm_g"][0])] * 4, row(f["b_sinks"][0][heads]),
        row(f["a_lambda_q1"][0]), row(f["a_lambda_k1"][0]), row(f["a_lambda_q2"][0]), row(f["a_lambda_k2"][0]),
    ], axis=1)
    ada_w = np.concatenate([f["a_ada_w"][0], f["kv_ada_w"], f["b_ada_w"][0]], axis=1)
    ada0_w = ada_w[:, :ADA0].reshape(KD, P, ADA0)
    ada1_w = ada_w[:, ADA0:].reshape(KD, P, A_HEADS, ADAW).transpose(2, 0, 1, 3)
    wa_in = f["a_w_in"][0].reshape(D, 4, A_HEADS, P).transpose(0, 2, 1, 3).reshape(D, 4 * D)
    w_a = np.concatenate([units(wa_in), units(f["a_w_out"][0])])
    wb_in = f["b_w_in"][0].reshape(D, 2, B_HEADS, HD)[:, :, heads].reshape(D, 2, B_UNITS, 256)
    wb_in = wb_in.transpose(0, 2, 1, 3).reshape(D, 2 * D)
    wb_out = f["b_w_out"][0].reshape(B_HEADS, HD, D)[heads].reshape(D, D)
    w_b = np.concatenate([units(wb_in), units(wb_out)])
    w_kv = f["w_kv"].reshape(KD, P, 256).transpose(1, 0, 2)
    arrays = {"x": f["x"][0], "par": par, "ada0_w": ada0_w, "ada1_w": ada1_w, "w_a": w_a, "w_kv": w_kv, "w_b": w_b}
    arrays = {k: np.ascontiguousarray(v) for k, v in arrays.items()}

    nc = bacc.Bacc("TRN2", target_bir_lowering=False, num_devices=1)
    args = [nc.dram_tensor(k, v.shape, F32, kind="ExternalInput").ap() for k, v in arrays.items()]
    args.append(nc.dram_tensor("h_out", (SEQ, D), F32, kind="ExternalOutput").ap())
    build(nc, *args)
    r = run_bass_kernel_spmd(nc, [arrays], core_ids=[0])
    return r.results[0]["h_out"].reshape(f["x"].shape)
```

```python
from contextlib import ExitStack

import numpy as np
import concourse.bass as bass
from concourse import mybir

F32 = mybir.dt.float32
F32R = mybir.dt.float32r
I32 = mybir.dt.int32
ALU = mybir.AluOpType
ACT = mybir.ActivationFunctionType
AX = mybir.AxisListType

P = 128
SEQ = 1024
D = 1024
NT = SEQ // P
KD = D // P
FW = 512
A_HEADS = 8
B_HEADS = 16
B_UNIT = 4
B_UNITS = B_HEADS // B_UNIT
HD = 64
EPS = 1e-6
LAMBDA_INIT = 0.8 - 0.6
MASKED = -1e30
HUGE = 3e38
ADA0 = 2048
ADAW = 768

C_VEC = 0
C_ADAB = C_VEC + KD
C_GA = C_ADAB + 64
C_GKV = C_GA + KD
C_GB = C_GKV + KD
C_AQK = C_GB + KD
C_SUB = C_AQK + 4 * HD
C_KVK = C_SUB + P
C_BQ = C_KVK + 2 * HD
C_SINK = C_BQ + 4 * HD
C_LAM = C_SINK + B_HEADS
N_PAR = C_LAM + 4 * HD

M_A_SHIFT, M_A_SCALE, M_A_GATE, M_KV_SHIFT, M_KV_SCALE, M_B_SHIFT, M_B_SCALE, M_B_GATE = range(0, 64, 8)


def slope_b(head):
    return float(np.float32(2.0 ** (-8.0 * (head + 1) / B_HEADS)))


def at_least(eng, sem, value):
    if not isinstance(value, int) or value > 0:
        eng.wait_ge(sem, value)


def stand_alone(eng, passed):
    eng.sem_inc(passed, 1)


def pipeline(eng, per, blocks, depth, slot):
    for i in range(per):
        slot(0, i, lambda lag, i=i: i >= lag)
    with eng.Fori(1, blocks) as blk:
        for i in range(per):
            slot(blk, i, lambda lag: True)
    for i in range(depth):
        slot(blocks, i, lambda lag, i=i: i < lag)


def score_base(it):
    return {4: 256, 5: 128, 6: 128}.get(it, 0)


def build(nc, x, par, ada0_w, ada1_w, w_a, w_kv, w_b, out):
    h1 = nc.dram_tensor("h1_scratch", [SEQ, D], F32).ap()
    o_a = nc.dram_tensor("oa_scratch", [SEQ, D], F32).ap()
    o_b = nc.dram_tensor("ob_scratch", [SEQ, D], F32).ap()

    ctx = ExitStack()
    with ctx:
        def sb(name, shape, dt=F32):
            return ctx.enter_context(nc.sbuf_tensor(name, shape, dt))

        def sem(name):
            return ctx.enter_context(nc.semaphore(name))

        u_hi = sb("u_hi", [P, KD, SEQ], F32R)
        u_lo = sb("u_lo", [P, KD, SEQ], F32R)
        w_hi = sb("w_hi", [P, KD, FW], F32R)
        w_lo = sb("w_lo", [P, KD, FW], F32R)
        raw = sb("raw", [P, KD, FW])
        kT = sb("kT", [P, 2, 2, SEQ], F32R)
        oT = kT[:, :, :, :].rearrange("p a b n -> p (a b) n")
        vs = sb("vs", [P, NT, 256], F32R)
        qT = sb("qT", [P, 2, 4 * P], F32R)
        p_hi = sb("p_hi", [P, 1024], F32R)
        p_lo = sb("p_lo", [P, 1024], F32R)
        split = sb("split", [P, 4 * 3 * HD], F32R)
        e0 = sb("e0", [P, 2, 1024])
        e1 = sb("e1", [P, 1024])
        stage = sb("stage", [P, 4, FW])
        qn = sb("qn", [P, 256])
        sq = sb("sq", [P, 256])
        bias = sb("bias", [P, 1024])
        ez = sb("ez", [P, 2, 256])
        zs = sb("zs", [P, 8, 256])
        ol = sb("ol", [P, 256])
        ob = sb("ob", [P, 2, 256])
        adabuf = sb("adabuf", [P, 3 * ADAW])
        ada_acc = adabuf[:, 0:ADAW]
        prm = sb("prm", [P, N_PAR])
        ident = sb("ident", [P, P])
        identr = sb("identr", [P, P], F32R)
        ones = sb("ones", [P, 1])
        mod = sb("mod", [P, 64])
        csil = sb("csil", [P, KD])
        cexp = sb("cexp", [P, KD])
        smod = sb("smod", [P, 3, KD])
        var = sb("var", [P, 8])
        y0 = sb("y0", [P, 8])
        ysq = sb("ysq", [P, 8])
        yh = sb("yh", [P, 8])
        rs = sb("rs", [P, 8])
        ssum = sb("ssum", [P, 8])
        oss = sb("oss", [P, 1])
        negm = sb("negm", [P, 2, 4])
        lsum = sb("lsum", [P, 4, 4])
        esnk = sb("esnk", [P, 4])
        nsink = sb("nsink", [P, 4])
        rl = sb("rl", [P, 4, 4])
        l1e = sb("l1e", [P, 2])
        lamt = sb("lamt", [P, 8])
        junk = sb("junk", [P, P])

        def ps(name, shape):
            return ctx.enter_context(nc.psum_tensor(name, shape, F32))

        ps_p = ps("ps_p", [P, 2, 512])
        ps_s = ps("ps_s", [P, 1024])
        ps_t = ps("ps_t", [P, 1024])
        ps_o = ps("ps_o", [P, 2, 512])

        s_par = sem("s_par")
        dve_passed = sem("dve_passed")
        pool_passed = sem("pool_passed")
        s_ident = sem("s_ident")
        s_const = sem("s_const")
        s_cexp = sem("s_cexp")
        s_lam = sem("s_lam")
        ada0_loaded = [sem(f"ada0_loaded{k}") for k in range(2)]
        ada0_used = sem("ada0_used")
        ada0_mm = sem("ada0_mm")
        s_mod = sem("s_mod")
        w_loaded = [sem(f"w_loaded{c}") for c in range(KD)]
        w_hi_done = sem("w_hi_done")
        w_lo_done = sem("w_lo_done")
        w_lo_pool = sem("w_lo_pool")
        w_free = sem("w_free")
        bias_a = sem("bias_a")
        bias_b = sem("bias_b")
        bias_step = sem("bias_step")
        n_x = [sem(f"n_x{k}") for k in range(2)]
        n_ss = sem("n_ss")
        n_var = sem("n_var")
        n_ln = sem("n_ln")
        n_y0 = sem("n_y0")
        n_step = sem("n_step")
        n_norm = sem("n_norm")
        n_tr = sem("n_tr")
        n_umod_d = sem("n_umod_d")
        n_umod_a = sem("n_umod_a")
        n_hi = sem("n_hi")
        u_ready = sem("u_ready")
        k_umod_d = sem("k_umod_d")
        k_umod_a = sem("k_umod_a")
        k_hi = sem("k_hi")
        k_lo = sem("k_lo")
        k_mm = sem("k_mm")
        k_raw = sem("k_raw")
        k_sq = sem("k_sq")
        k_sum = sem("k_sum")
        k_var = sem("k_var")
        k_ln = sem("k_ln")
        k_y0 = sem("k_y0")
        k_step = sem("k_step")
        k_kn = sem("k_kn")
        k_shi = sem("k_shi")
        k_split = sem("k_split")
        k_tr = sem("k_tr")
        k_kT = sem("k_kT")
        k_vhi = sem("k_vhi")
        k_v = sem("k_v")
        c_o = [sem(f"c_o{k}") for k in range(2)]
        c_res = [sem(f"c_res{k}") for k in range(2)]
        c_tr = sem("c_tr")
        c_hi = sem("c_hi")
        c_lo = sem("c_lo")
        c_mm = sem("c_mm")
        c_y = sem("c_y")
        c_sum = sem("c_sum")
        c_st = [sem(f"c_st{k}") for k in range(2)]
        g_cols = sem("g_cols")
        g_mm = sem("g_mm")
        g_tab = sem("g_tab")

        class AttnSems:

            def __init__(self, pre):
                self.proj = sem(pre + "proj")
                self.staged = sem(pre + "staged")
                self.sq = sem(pre + "sq")
                self.ssum = sem(pre + "ssum")
                self.var = sem(pre + "var")
                self.ln = sem(pre + "ln")
                self.y0 = sem(pre + "y0")
                self.step = sem(pre + "step")
                self.rs = sem(pre + "rs")
                self.qn = sem(pre + "qn")
                self.shi = sem(pre + "shi")
                self.split = sem(pre + "split")
                self.tr = sem(pre + "tr")
                self.qkT = sem(pre + "qkT")
                self.s = sem(pre + "s")
                self.m = sem(pre + "m")
                self.e = sem(pre + "e")
                self.ratio = sem(pre + "ratio")
                self.comb = sem(pre + "comb")
                self.pt = sem(pre + "pt")
                self.phi = sem(pre + "phi")
                self.plo = sem(pre + "plo")
                self.pv = sem(pre + "pv")
                self.ol = sem(pre + "ol")
                self.oadd = sem(pre + "oadd")
                self.oss = sem(pre + "oss")
                self.fin = sem(pre + "fin")
                self.st = [sem(f"{pre}st{k}") for k in range(2)]
                self.ez = sem(pre + "ez")
                self.z1 = sem(pre + "z1")
                self.zr = sem(pre + "zr")
                self.zg = sem(pre + "zg")
                self.vhi = sem(pre + "vhi")
                self.v = sem(pre + "v")
                self.tab = sem(pre + "tab")

        a = AttnSems("a_")
        b = AttnSems("b_")
        b_snk = sem("b_snk")
        b_esnk = sem("b_esnk")
        b_nsink = sem("b_nsink")
        ada_loaded = [sem(f"ada_loaded{k}") for k in range(2)]
        ada_scaled = sem("ada_scaled")
        ada_acc_done = sem("ada_acc_done")
        ada_mm = sem("ada_mm")

        block = ctx.enter_context(nc.Block())

        U_OUT_A, U_KV, U_B, U_OUT_B = A_HEADS, A_HEADS + 2, A_HEADS + 3, A_HEADS + 3 + B_UNITS
        POOL_LO = 4
        DVE_LO = KD - POOL_LO

        def low_ready(eng, unit, unit_a, c):
            if c < DVE_LO:
                eng.wait_ge(w_lo_done, 8 * unit + c + 1)
            else:
                eng.wait_ge(w_lo_pool, POOL_LO * unit_a + c - DVE_LO + 1)
        V_KV, V_B = A_HEADS, A_HEADS + 1

        @block.sync
        def _(sp):
            sp.dma_start(prm[:, :], par).then_inc(s_par, 16)
            big = [e0[:, :, :].rearrange("p a n -> p (a n)"), stage[:, :, :].rearrange("p a n -> p (a n)")]
            for c in range(KD):
                at_least(sp, ada0_used, c - 1)
                sp.dma_start(big[c % 2], ada0_w[c]).then_inc(ada0_loaded[c % 2], 16)
            for c in range(KD):
                sp.dma_start(raw[:, c, :], w_a[0, :, c, :]).then_inc(w_loaded[c], 16)

            def norm_loads(src, n0, stores):
                def slot(blk, i, live):
                    n = 4 * blk + i
                    if not live(0) or (stores and isinstance(blk, int) and blk == 0 and i < 2):
                        return
                    if stores:
                        sp.wait_ge(c_st[i % 2], 16 * (2 * blk + i // 2 + 1))
                    at_least(sp, n_tr, n + n0 - 1)
                    sp.dma_start(e0[:, i % 2, :], src[bass.ds(n * P, P), :]).then_inc(n_x[i % 2], 16)
                pipeline(sp, 4, NT // 4, 0, slot)

            def attn_io(S, units, w_src, unit0, unit_a0, width, o_dram, with_ada):
                def slot(u, i, live):
                    if not live(0) and 1 <= i <= 4:
                        for c in (2 * i - 2, 2 * i - 1):
                            sp.wait_ge(w_lo_done, 8 * (units + unit0) + c + 1)
                            sp.dma_start(raw[:, c, :], w_src[units + 1, :, c, :]).then_inc(w_loaded[c], 16)
                    if not live(0) and i == 4:
                        sp.wait_ge(S.pt, units * NT)
                        for k in range(2):
                            sp.wait_ge(S.st[k], 16 * ((units - 1) * NT // 2 + 1))
                            sp.dma_start(e0[:, k, :], o_dram[k * P:(k + 1) * P, :]).then_inc(c_o[k], 16)
                    if with_ada and live(0):
                        at_least(sp, ada_acc_done, 8 * u + i - 1)
                        sp.dma_start(adabuf[:, ADAW * (1 + i % 2):ADAW * (2 + i % 2)],
                                     ada1_w[u, i, :, :]).then_inc(ada_loaded[i % 2], 16)
                    if live(0) and i >= 2:
                        for c in {2: (0, 1), 3: (2, 3), 4: (4, 5), 5: (6, 7)}.get(i, ()):
                            low_ready(sp, u + unit0, u + unit_a0, c)
                            sp.dma_start(raw[:, c, :], w_src[u + 1, :, c, :]).then_inc(w_loaded[c], 16)
                    if live(6):
                        it = (i - 6) % 8
                        ub = u + (i - 6) // 8
                        sp.wait_ge(S.fin, 8 * u + i - 6 + 1)
                        sp.dma_start(o_dram[it * P:(it + 1) * P, bass.ds(ub * width, width)],
                                     ob[:, it % 2, 0:width]).then_inc(S.st[it % 2], 16)
                pipeline(sp, 8, units, 6, slot)

            def out_io(S, units, res_src, o_dram, dst, n0, early, late):
                def slot(blk, i, live):
                    n = 2 * blk + i
                    if live(0) and not isinstance(blk, int):
                        at_least(sp, c_tr, n + n0 - 1)
                        sp.wait_ge(S.st[i], 16 * (blk + (units - 1) * NT // 2 + 1))
                        sp.dma_start(e0[:, i, :], o_dram[bass.ds(n * P, P), :]).then_inc(c_o[i], 16)
                    if live(1):
                        j = (i - 1) % 2
                        if isinstance(blk, int) and blk == 0:
                            for k in range(2):
                                sp.wait_ge(S.st[k], 16 * units * NT // 2)
                        elif not isinstance(blk, int) or i >= 1 or blk:
                            sp.wait_ge(c_sum, n + n0 - 2)
                        sp.dma_start(stage[:, 2 * j:2 * j + 2, :].rearrange("p a n -> p (a n)"),
                                     res_src[bass.ds((n - 1) * P, P), :]).then_inc(c_res[j], 16)
                    if live(2):
                        j = i % 2
                        sp.wait_ge(c_sum, n + n0 - 1)
                        sp.dma_start(dst[bass.ds((n - 2) * P, P), :],
                                     adabuf[:, j * D:(j + 1) * D]).then_inc(c_st[j], 16)
                    if isinstance(blk, int) and blk == 0 and i == 1:
                        early()
                    if not live(0) and i == 0:
                        late()
                pipeline(sp, 2, NT // 2, 2, slot)

            sp.wait_ge(ada0_used, KD)
            norm_loads(x, 0, False)
            sp.wait_ge(ada0_mm, 1)
            attn_io(a, A_HEADS, w_a, 0, 0, P, o_a, True)

            def kv_weights():
                for c in range(KD):
                    sp.wait_ge(w_lo_done, 8 * (U_OUT_A + 1) + c + 1)
                    sp.dma_start(raw[:, c, 0:256], w_kv[:, c, :]).then_inc(w_loaded[c], 16)

            def next_layer():
                sp.wait_ge(c_tr, NT)
                for k in range(2):
                    sp.wait_ge(c_st[k], 16)
                    sp.dma_start(e0[:, k, :], h1[k * P:(k + 1) * P, :]).then_inc(n_x[k], 16)
                for c in range(KD):
                    sp.wait_ge(w_lo_done, 8 * U_KV + c + 1)
                    sp.dma_start(raw[:, c, :], w_b[0, :, c, :]).then_inc(w_loaded[c], 16)

            out_io(a, A_HEADS, x, o_a, h1, 0, kv_weights, next_layer)
            norm_loads(h1, NT, True)
            attn_io(b, B_UNITS, w_b, U_B, A_HEADS, 256, o_b, False)
            out_io(b, B_UNITS, h1, o_b, out, NT, lambda: None, lambda: None)
            for k in range(2):
                sp.wait_ge(c_st[k], 16 * NT)

        @block.gpsimd
        def _(pool):
            pool.memset(ident[:, :], 0.0).then_inc(s_ident, 1)
            pool.wait_ge(s_ident, 1)
            pool.affine_select(out=ident[:, :], in_=ident[:, :], compare_op=ALU.not_equal, fill=1.0, base=0,
                               pattern=[[-1, P]], channel_multiplier=1).then_inc(s_ident, 1)
            pool.wait_ge(s_ident, 2)
            pool.tensor_copy(identr[:, :], ident[:, :]).then_inc(s_ident, 1)
            pool.iota(e1[:, :].bitcast(I32), pattern=[[1, 1024]], base=-896, channel_multiplier=-1).then_inc(bias_step, 1)
            pool.wait_ge(bias_step, 1)
            pool.tensor_copy(bias[:, :], e1[:, :].bitcast(I32)).then_inc(bias_step, 1)
            pool.wait_ge(bias_step, 2)
            pool.tensor_scalar(bias[:, :], bias[:, :], 0.5, 1.0, ALU.mult, ALU.mult).then_inc(bias_step, 1)
            pool.wait_ge(bias_step, 3)
            pool.affine_select(out=bias[:, :], in_=bias[:, :], compare_op=ALU.is_ge, fill=MASKED, base=896,
                               pattern=[[-1, 1024]], channel_multiplier=1).then_inc(bias_a, 1)

            def last_chunks_low(unit):
                for c in range(DVE_LO, KD):
                    pool.wait_ge(w_hi_done, 8 * unit + c + 1)
                    pool.tensor_tensor(w_lo[:, c, :], raw[:, c, :], w_hi[:, c, :].bitcast(F32),
                                       ALU.subtract).then_inc(w_lo_pool, 1)

            def attn(S, units, u0, unit_a0, zw, is_a):
                zc = FW - zw

                def slot(u, i, live):
                    s = 8 * u + i
                    if live(2):
                        n = s - 2
                        it = (i - 2) % 8
                        st = stage[:, it % 4, :]
                        pool.wait_ge(S.staged, n + 1)
                        pool.wait_ge(S.ez, n + 1)
                        if is_a:
                            pool.tensor_tensor(st[:, zc:FW], st[:, zc:FW], prm[:, C_SUB:C_SUB + P], ALU.mult)
                        stand_alone(pool, pool_passed)
                        pool.tensor_scalar(ez[:, i % 2, 0:zw], ez[:, i % 2, 0:zw], 1.0, 1.0, ALU.add, ALU.mult).then_inc(S.z1, 1)
                    if live(0) and i == 1 and not (isinstance(u, int) and u == 0):
                        last_chunks_low(u + u0)
                    if is_a and live(4):
                        n = s - 4
                        it = (i - 4) % 8
                        st = stage[:, it % 4, :]
                        pool.wait_ge(S.vhi, n + 1)
                        pool.tensor_tensor(vs[:, it, P:256], st[:, 256:384], vs[:, it, 0:P].bitcast(F32),
                                           ALU.subtract).then_inc(S.v, 1)
                    if live(2):
                        n = s - 2
                        st = stage[:, (i - 2) % 4, :]
                        pool.wait_ge(S.zr, n + 1)
                        pool.tensor_tensor(zs[:, (i - 2) % 8, 0:zw], st[:, zc:FW], ez[:, i % 2, 0:zw], ALU.mult).then_inc(S.zg, 1)
                    if live(0) and is_a:
                        src = adabuf[:, ADAW * (1 + i % 2):ADAW * (2 + i % 2)]
                        pool.wait_ge(ada_loaded[i % 2], 16 * (4 * u + i // 2 + 1))
                        at_least(pool, ada_acc_done, 8 * u + i)
                        if i == 0:
                            at_least(pool, ada_mm, u)
                            stand_alone(pool, pool_passed)
                            pool.tensor_scalar(ada_acc, src, csil[:, 0:1], 1.0, ALU.mult, ALU.mult).then_inc(ada_acc_done, 1)
                        else:
                            stand_alone(pool, pool_passed)
                            pool.tensor_scalar(src, src, csil[:, i:i + 1], 1.0, ALU.mult, ALU.mult).then_inc(ada_scaled, 1)
                            pool.wait_ge(ada_scaled, 7 * u + i)
                            pool.tensor_tensor(ada_acc, ada_acc, src, ALU.add).then_inc(ada_acc_done, 1)
                pipeline(pool, 8, units, 6, slot)

            def out_sums(n0):
                def slot(blk, i, live):
                    if live(1):
                        n = 2 * blk + i - 1 + n0
                        j = (i - 1) % 2
                        yo = adabuf[:, j * D:(j + 1) * D]
                        pool.wait_ge(c_y, 2 * n + 2)
                        pool.wait_ge(c_res[j], 16 * (blk + n0 // 2 + (1 if j == 0 else 0)))
                        pool.tensor_tensor(yo, yo, stage[:, 2 * j:2 * j + 2, :].rearrange("p a n -> p (a n)"),
                                           ALU.add).then_inc(c_sum, 1)
                pipeline(pool, 2, NT // 2, 1, slot)

            last_chunks_low(0)
            pool.wait_ge(s_const, 3)
            pool.wait_ge(s_lam, 4)
            pool.wait_ge(ada0_mm, 1)
            attn(a, A_HEADS, 0, 0, P, True)
            pool.wait_ge(a.m, 2 * A_HEADS * NT)
            pool.wait_ge(a.comb, A_HEADS * NT)
            pool.iota(qn[:, :].bitcast(I32), pattern=[[1, 256]], base=-P, channel_multiplier=-1).then_inc(bias_step, 1)
            pool.wait_ge(bias_step, 4)
            for j, head in enumerate((0, 1, 8, 9)):
                pool.tensor_copy(bias[:, 256 * j:256 * j + 256], qn[:, :].bitcast(I32)).then_inc(bias_step, 1)
            pool.wait_ge(bias_step, 8)
            for j, head in enumerate((0, 1, 8, 9)):
                pool.tensor_scalar(bias[:, 256 * j:256 * j + 256], bias[:, 256 * j:256 * j + 256],
                                   slope_b(head), 1.0, ALU.mult, ALU.mult).then_inc(bias_step, 1)
            pool.wait_ge(bias_step, 12)
            pool.affine_select(out=bias[:, :], in_=bias[:, :], compare_op=ALU.is_ge, fill=MASKED, base=P,
                               pattern=[[0, 4], [-1, 256]], channel_multiplier=1).then_inc(bias_step, 1)
            pool.wait_ge(bias_step, 13)
            pool.affine_select(out=bias[:, :], in_=bias[:, :], compare_op=ALU.is_ge, fill=MASKED, base=-1,
                               pattern=[[0, 4], [1, 256]], channel_multiplier=-1).then_inc(bias_b, 1)
            out_sums(0)

            def kv_slot(blk, i, live):
                if live(3):
                    n = 4 * blk + i - 3
                    pool.wait_ge(k_raw, n + 1)
                    at_n = vs[:, bass.ds(n, 1), :].rearrange("p o (g c) -> p (o g) c", c=P)
                    v_raw = ol[:, P:256].rearrange("p (g c) -> p g c", c=HD)
                    stand_alone(pool, pool_passed)
                    pool.tensor_copy(at_n[:, :, 0:HD], v_raw).then_inc(k_vhi, 1)
                    pool.wait_ge(k_vhi, n + 1)
                    pool.tensor_tensor(at_n[:, :, HD:P], v_raw, at_n[:, :, 0:HD].bitcast(F32),
                                       ALU.subtract).then_inc(k_v, 1)
            pipeline(pool, 4, NT // 4, 3, kv_slot)
            attn(b, B_UNITS, U_B, A_HEADS, 256, False)
            out_sums(NT)

        @block.tensor
        def _(pe):
            def adaln_first():
                pe.wait_ge(s_const, 4)
                pe.wait_ge(ada0_used, KD)
                for j in range(ADA0 // P):
                    mm = pe.matmul(ps_p[:, 0, j:j + 1], adabuf[:, j * P:(j + 1) * P], ones[:, :], start=True, stop=True)
                mm.then_inc(ada0_mm, 1)

            def project(S, is_a, u, it, n, chunks):
                o = ps_p[:, it % 2, :]
                if not len(chunks):
                    return
                if chunks[0] == 0:
                    at_least(pe, S.staged, n - 1)
                if isinstance(u, int) and u == 0 and chunks[0] == 0:
                    pe.wait_ge(u_ready, (0 if is_a else NT) + it + 1)
                    if not is_a and it == 1:
                        pe.wait_ge(k_kT, NT)
                        pe.wait_ge(k_v, NT)
                for c in chunks:
                    if it == 0:
                        low_ready(pe, u + (0 if is_a else U_B), u + (0 if is_a else A_HEADS), c)
                    t = slice(it * P, (it + 1) * P)
                    pe.matmul(o, u_hi[:, c, t], w_hi[:, c, :], start=(c == 0), stop=False)
                    pe.matmul(o, u_hi[:, c, t], w_lo[:, c, :], start=False, stop=False)
                    mm = pe.matmul(o, u_lo[:, c, t], w_hi[:, c, :], start=False, stop=(c == KD - 1))
                    if it == NT - 1 and c < KD - 1:
                        mm.then_inc(w_free, 1)
                if chunks[-1] == KD - 1:
                    mm.then_inc(S.proj, 1)
                    if it == NT - 1:
                        pe.wait_ge(S.proj, n + 1)
                        pe.nop().then_inc(w_free, 1)

            def norm(n0, with_kv):
                def slot(blk, i, live):
                    s = 4 * blk + i
                    if live(1):
                        n = s - 1
                        j = (i - 1) % 2
                        dst = (ps_t, ps_s)[j]
                        pe.wait_ge(n_norm, n + n0 + 1)
                        at_least(pe, n_umod_d, n + n0 - 1)
                        at_least(pe, n_umod_a, n + n0 - 1)
                        if with_kv:
                            at_least(pe, k_umod_d, n - 1)
                            at_least(pe, k_umod_a, n - 1)
                        for d in range(KD):
                            mm = pe.transpose(dst[:, d * P:(d + 1) * P], e0[:, j, d * P:(d + 1) * P], ident[:, :])
                        mm.then_inc(n_tr, 1)
                    if with_kv and live(4):
                        n = s - 4
                        pe.wait_ge(k_split, n + 1)
                        at_least(pe, k_kT, n)
                        for g in range(2):
                            for o in range(2):
                                mm = pe.transpose(ps_p[:, 1, (2 * g + o) * P:(2 * g + o + 1) * P].bitcast(F32R),
                                                  split[:, g * 192 + o * HD:g * 192 + o * HD + P], identr[:, :])
                        mm.then_inc(k_tr, 1)
                    if with_kv and live(2):
                        n = s - 2
                        it = (i - 2) % 4
                        last = isinstance(blk, int) and blk == NT // 4 and i == 1
                        pe.wait_ge(k_lo, n + 1)
                        at_least(pe, k_raw, n - 1)
                        for c in range(KD):
                            if isinstance(blk, int) and blk == 0 and i == 2:
                                pe.wait_ge(w_lo_done, 8 * U_KV + c + 1)
                            st_hi, st_lo = p_hi[:, c * P:(c + 1) * P], p_lo[:, c * P:(c + 1) * P]
                            o = ps_o[:, it % 2, 0:256]
                            pe.matmul(o, st_hi, w_hi[:, c, 0:256], start=(c == 0), stop=False)
                            pe.matmul(o, st_hi, w_lo[:, c, 0:256], start=False, stop=False)
                            mm = pe.matmul(o, st_lo, w_hi[:, c, 0:256], start=False, stop=(c == KD - 1))
                            if last and c < KD - 1:
                                mm.then_inc(w_free, 1)
                        mm.then_inc(k_mm, 1)
                        if last:
                            pe.wait_ge(k_mm, NT)
                            pe.nop().then_inc(w_free, 1)
                    if not n0 and isinstance(blk, int) and blk == 1 and live(0) and i >= 2:
                        project(a, True, 0, i - 2, i - 2, range(KD))
                pipeline(pe, 4, NT // 4, 4 if with_kv else 1, slot)

            def gate_rows(k):
                pe.wait_ge(g_cols, k + 1)
                for d in range(KD):
                    mm = pe.matmul(ps_s[:, d * P:(d + 1) * P], adabuf[:, d * P:(d + 1) * P], ident[:, :],
                                   start=True, stop=True)
                mm.then_inc(g_mm, 1)

            def attn(S, units, is_a, gate):
                def scores_a(sub, it, n):
                    if sub == 0:
                        pe.wait_ge(S.qkT, n + 1)
                    at_least(pe, S.m, 2 * n + sub)
                    base, nk = score_base(it), (it + 1) * P
                    cuts = [0, nk] if nk <= 512 else [0, 512 - base, nk]
                    for lo_k, hi_k in zip(cuts, cuts[1:]):
                        for o in range(2):
                            mm = pe.matmul(ps_s[:, base + lo_k:base + hi_k], qT[:, it % 2, sub * P:(sub + 1) * P],
                                           kT[:, sub, o, lo_k:hi_k], start=(o == 0), stop=(o == 1))
                    mm.then_inc(S.s, 1)

                def scores_b(part, it, n):
                    if part == 0:
                        pe.wait_ge(S.qkT, n + 1)
                    at_least(pe, S.m, 2 * (n - 1) + part + 1)
                    w0 = P if it == 0 else 0
                    for j in (2 * part, 2 * part + 1):
                        for o in range(2):
                            mm = pe.matmul(ps_s[:, j * 256 + w0:j * 256 + 256], qT[:, it % 2, j * P:(j + 1) * P],
                                           kT[:, j // 2, o, (it - 1) * P + w0:(it + 1) * P],
                                           start=(o == 0), stop=(o == 1))
                    mm.then_inc(S.s, 1)

                scores = scores_a if is_a else scores_b

                def slot(u, i, live):
                    s = 8 * u + i
                    n1, n3, n4, n5 = s - 1, s - 3, s - 4, s - 5
                    i1, i3, i4, i5 = (i - 1) % 8, (i - 3) % 8, (i - 4) % 8, (i - 5) % 8
                    u1 = u + (i - 1) // 8
                    late = KD - 1
                    projected = is_a and isinstance(u, int) and u == 0 and i in (1, 2)
                    if live(4):
                        scores(0, i4, n4)
                        if not is_a:
                            scores(1, i4, n4)
                    if live(1) and not projected:
                        project(S, is_a, u1, i1, n1, range(0, 2))
                    if live(4) and is_a:
                        scores(1, i4, n4)
                    if not live(0) and i == 4:
                        pe.wait_ge(S.m, 2 * units * NT)
                        gate_rows(gate)
                    if live(5):
                        pe.wait_ge(S.phi, n5 + 1)
                        pe.wait_ge(S.plo, n5 + 1)
                        if is_a:
                            pe.wait_ge(S.v, n5 + 1)
                            at_least(pe, S.oadd, n5 - 1)
                            if i == 2 and live(10):
                                pe.wait_ge(s_mod, 3 + u)
                            o = ps_o[:, i5 % 2, :]
                            for j in range(i5 + 1):
                                pe.matmul(o[:, 0:256], p_hi[:, j * P:(j + 1) * P], vs[:, j, :], start=(j == 0), stop=False)
                                mm = pe.matmul(o[:, 0:256], p_lo[:, j * P:(j + 1) * P], vs[:, j, :], start=False,
                                               stop=(j == i5))
                        else:
                            at_least(pe, S.oadd, n5)
                            for j in range(4):
                                o = ps_o[:, j // 2, (j % 2) * 256:(j % 2) * 256 + 256]
                                first = 1 if i5 == 0 else 0
                                for k in range(first, 2):
                                    t = slice((2 * j + k) * P, (2 * j + k + 1) * P)
                                    pe.matmul(o, p_hi[:, t], vs[:, i5 - 1 + k, :], start=(k == first), stop=False)
                                    mm = pe.matmul(o, p_lo[:, t], vs[:, i5 - 1 + k, :], start=False, stop=(k == 1))
                        mm.then_inc(S.pv, 1)
                    if live(3):
                        pe.wait_ge(S.split, n3 + 1)
                        if is_a:
                            for sub in range(2):
                                for o in range(2):
                                    c = (2 + sub) * 192 + o * HD
                                    pe.transpose(ps_t[:, (2 * sub + o) * P:(2 * sub + o + 1) * P].bitcast(F32R),
                                                 split[:, c:c + P], identr[:, :])
                            for sub in range(2):
                                mm = pe.transpose(ps_t[:, 512 + sub * P:512 + (sub + 1) * P].bitcast(F32R),
                                                  split[:, sub * 192:sub * 192 + P], identr[:, :])
                        else:
                            for j in range(4):
                                mm = pe.transpose(ps_t[:, j * P:(j + 1) * P].bitcast(F32R),
                                                  split[:, j * 192:j * 192 + P], identr[:, :])
                        mm.then_inc(S.tr, 1)
                    if live(1) and not projected:
                        project(S, is_a, u1, i1, n1, range(2, late))
                    if live(4):
                        pe.wait_ge(S.comb if is_a else S.e, n4 + 1 if is_a else 2 * n4 + 2)
                        if live(3):
                            pe.wait_ge(S.qkT, n3 + 1)
                        if is_a:
                            for j in range(i4 + 1):
                                mm = pe.transpose(ps_t[:, j * P:(j + 1) * P], e0[:, i4 % 2, j * P:(j + 1) * P], ident[:, :])
                        else:
                            for j in range(8):
                                if i4 > 0 or j % 2 == 1:
                                    mm = pe.transpose(ps_t[:, j * P:(j + 1) * P], e0[:, i4 % 2, j * P:(j + 1) * P],
                                                      ident[:, :])
                        mm.then_inc(S.pt, 1)
                    if live(1) and not projected:
                        project(S, is_a, u1, i1, n1, range(late, KD))
                    if is_a and i == 0 and live(8):
                        pe.wait_ge(ada_acc_done, 8 * u)
                        pe.wait_ge(S.oadd, n5 + 1)
                        for j in range(ADAW // P):
                            mm = pe.matmul(ps_o[:, i5 % 2, 500 + j:501 + j], ada_acc[:, j * P:(j + 1) * P], ones[:, :],
                                           start=True, stop=True)
                        mm.then_inc(ada_mm, 1)
                pipeline(pe, 8, units, 6, slot)

            def output(n0, u0):
                def slot(blk, i, live):
                    def half(h):
                        n = 2 * blk + i - 1 + n0
                        j = (i - 1) % 2
                        if h == 0:
                            pe.wait_ge(c_lo, n + 1)
                            at_least(pe, c_y, 2 * (n - 2) + 2)
                        o = (ps_p, ps_o)[j][:, h, :]
                        for c in range(KD):
                            if isinstance(blk, int) and blk == 0:
                                pe.wait_ge(w_lo_done, 8 * (u0 + h) + c + 1)
                            hi = oT[:, 2 * j, c * P:(c + 1) * P]
                            lo = oT[:, 2 * j + 1, c * P:(c + 1) * P]
                            f = slice(h * FW, (h + 1) * FW)
                            pe.matmul(o, hi, u_hi[:, c, f], start=(c == 0), stop=False)
                            pe.matmul(o, hi, u_lo[:, c, f], start=False, stop=False)
                            mm = pe.matmul(o, lo, u_hi[:, c, f], start=False, stop=(c == KD - 1))
                        mm.then_inc(c_mm, 1)

                    if live(1):
                        half(0)
                    if live(0):
                        n = 2 * blk + i + n0
                        pe.wait_ge(c_o[i], 16 * (blk + n0 // 2 + 1))
                        at_least(pe, c_lo, n)
                        for d in range(KD):
                            mm = pe.transpose(ps_t[:, d * P:(d + 1) * P], e0[:, i, d * P:(d + 1) * P], ident[:, :])
                        mm.then_inc(c_tr, 1)
                    if live(1):
                        half(1)
                pipeline(pe, 2, NT // 2, 1, slot)

            pe.wait_ge(s_ident, 3)
            adaln_first()
            norm(0, False)
            attn(a, A_HEADS, True, 0)
            output(0, U_OUT_A)
            norm(NT, True)
            attn(b, B_UNITS, False, 1)
            output(NT, U_OUT_B)

        @block.scalar
        def _(act):
            def split_hi(unit, c, dst, free_at, width=FW):
                act.wait_ge(w_loaded[c], 16 * (unit + 1))
                at_least(act, w_free, free_at)
                act.activation(dst, raw[:, c, 0:width], ACT.Copy).then_inc(w_hi_done, 1)

            def norm(n0, with_kv):
                def slot(blk, i, live):
                    s = 4 * blk + i
                    n1, n3, n4 = s - 1, s - 3, s - 4
                    if live(0):
                        act.wait_ge(n_x[i % 2], 16 * (2 * blk + n0 // 2 + i // 2 + 1))
                        at_least(act, n_var, s + n0)
                        at_least(act, n_ss, s + n0)
                        if n0 and isinstance(blk, int) and blk == 0 and i == 0:
                            act.wait_ge(c_sum, NT - 1)
                        act.activation(stage[:, 0:2, :].rearrange("p a n -> p (a n)"), e0[:, i % 2, :], ACT.Square,
                                       accum_out=ssum[:, 0:1]).then_inc(n_ss, 1)
                    if with_kv and live(3):
                        act.wait_ge(k_mm, n3 + 1)
                        at_least(act, k_v, n3)
                        at_least(act, k_kn, n3)
                        act.activation(ol[:, :], ps_o[:, (i - 3) % 2, 0:256], ACT.Copy).then_inc(k_raw, 1)
                    if live(1):
                        src = (ps_t, ps_s)[(i - 1) % 2]
                        if n0 and isinstance(blk, int) and blk == 0 and i == 1:
                            act.wait_ge(c_sum, NT)
                        act.wait_ge(n_tr, n1 + n0 + 1)
                        at_least(act, u_ready, n1 + n0)
                        k, shift = (2, M_B_SHIFT) if with_kv else (0, M_A_SHIFT)
                        for d in range(4, KD):
                            last = act.activation(e1[:, d * P:(d + 1) * P], src[:, d * P:(d + 1) * P], ACT.Identity,
                                                  scale=smod[:, k, d:d + 1], bias=mod[:, shift + d:shift + d + 1])
                        last.then_inc(n_umod_a, 1)
                        if with_kv:
                            at_least(act, k_lo, n1)
                            for d in range(4, KD):
                                last = act.activation(stage[:, 2 + d // 4, (d % 4) * P:(d % 4 + 1) * P],
                                                      src[:, d * P:(d + 1) * P], ACT.Identity,
                                                      scale=smod[:, 1, d:d + 1],
                                                      bias=mod[:, M_KV_SHIFT + d:M_KV_SHIFT + d + 1])
                            last.then_inc(k_umod_a, 1)
                    if with_kv and live(4):
                        act.wait_ge(k_tr, n4 + 1)
                        act.activation(kT[:, :, :, bass.ds(n4 * P, P)].rearrange("p a b t -> p (a b) t"),
                                       ps_p[:, 1, :].rearrange("p (g t) -> p g t", t=P), ACT.Copy).then_inc(k_kT, 1)
                    if live(0):
                        act.wait_ge(n_var, s + n0 + 1)
                        act.activation(y0[:, 0:1], var[:, 0:1], ACT.Ln).then_inc(n_ln, 1)
                        act.wait_ge(n_ln, s + n0 + 1)
                        act.activation(y0[:, 0:1], y0[:, 0:1], ACT.Exp, scale=-0.5).then_inc(n_y0, 1)
                    if with_kv and live(3):
                        act.wait_ge(k_var, n3 + 1)
                        act.activation(y0[:, 4:6], var[:, 4:6], ACT.Ln).then_inc(k_ln, 1)
                        act.wait_ge(k_ln, n3 + 1)
                        act.activation(y0[:, 4:6], y0[:, 4:6], ACT.Exp, scale=-0.5).then_inc(k_y0, 1)
                    if live(1):
                        act.wait_ge(n_umod_d, n1 + n0 + 1)
                        act.wait_ge(n_umod_a, n1 + n0 + 1)
                        if n0:
                            if isinstance(blk, int) and blk == 0 and i == 1:
                                act.wait_ge(c_mm, 2 * NT)
                        act.activation(u_hi[:, :, bass.ds(n1 * P, P)], e1[:, :].rearrange("p (d t) -> p d t", t=P),
                                       ACT.Copy).then_inc(n_hi, 1)
                        if with_kv:
                            act.wait_ge(k_umod_d, n1 + 1)
                            act.wait_ge(k_umod_a, n1 + 1)
                            at_least(act, k_mm, n1)
                            act.activation(p_hi[:, :], stage[:, 2:4, :].rearrange("p a n -> p (a n)"),
                                           ACT.Copy).then_inc(k_hi, 1)
                    if not n0 and isinstance(blk, int) and blk == 0:
                        for c in (2 * i, 2 * i + 1):
                            split_hi(0, c, w_hi[:, c, :], 0)
                    if with_kv and live(3):
                        act.wait_ge(k_kn, n3 + 1)
                        at_least(act, k_tr, n3)
                        act.activation(split[:, 0:384].rearrange("p (g c) -> p g c", c=192)[:, :, 0:HD],
                                       qn[:, 0:P].rearrange("p (g c) -> p g c", c=HD), ACT.Copy).then_inc(k_shi, 1)
                    if n0 and not live(0) and i in (1, 2):
                        for c in range(4 * i - 4, 4 * i):
                            split_hi(U_B, c, w_hi[:, c, :], 8 * V_KV + c + 1)
                pipeline(act, 4, NT // 4, 4, slot)

            def attn(S, units, v0, u0, is_a):
                zw = P if is_a else 256

                def exps(part, it, n):
                    act.wait_ge(S.m, 2 * n + part + 1)
                    ring = it % 4
                    if is_a:
                        e = e0[:, it % 2, 0:(it + 1) * P] if part == 0 else e1[:, 0:(it + 1) * P]
                        act.activation(e, e, ACT.Exp, scale=-1.0, bias=negm[:, it % 2, part:part + 1],
                                       accum_out=lsum[:, ring, part:part + 1]).then_inc(S.e, 1)
                    else:
                        w0 = P if it == 0 else 0
                        for j in (2 * part, 2 * part + 1):
                            e = e0[:, it % 2, j * 256 + w0:j * 256 + 256]
                            last = act.activation(e, e, ACT.Exp, scale=-1.0, bias=negm[:, it % 2, j:j + 1],
                                                  accum_out=lsum[:, ring, j:j + 1])
                        last.then_inc(S.e, 1)

                def slot(u, i, live):
                    s = 8 * u + i
                    n2, n3, n4, n5 = s - 2, s - 3, s - 4, s - 5
                    i2, i3, i4, i5 = (i - 2) % 8, (i - 3) % 8, (i - 4) % 8, (i - 5) % 8

                    def split_next(chunks):
                        if isinstance(u, int) and u == 0:
                            return
                        for c in chunks:
                            split_hi(u + u0, c, w_hi[:, c, :], 8 * (u + v0 - 1) + c + 1)
                    def second_part():
                        if live(4):
                            exps(1, i4, n4)
                            if not is_a:
                                act.wait_ge(b_snk, n4 + 1)
                                act.activation(esnk[:, :], esnk[:, :], ACT.Exp).then_inc(b_esnk, 1)

                    if live(2):
                        act.wait_ge(S.proj, n2 + 1)
                        at_least(act, S.ssum, n2)
                        act.activation(sq[:, :], ps_p[:, i2 % 2, 0:256], ACT.Square).then_inc(S.sq, 1)
                        at_least(act, S.zg, n2 - 1)
                        if is_a:
                            at_least(act, S.v, n2 - 3)
                        act.activation(stage[:, i2 % 4, :], ps_p[:, i2 % 2, :], ACT.Copy).then_inc(S.staged, 1)
                        act.wait_ge(S.staged, n2 + 1)
                        act.activation(ez[:, i2 % 2, 0:zw], stage[:, i2 % 4, FW - zw:FW], ACT.Exp, scale=-1.0).then_inc(S.ez, 1)
                    if live(0) and i == 1:
                        split_next((4,))
                    if live(4):
                        exps(0, i4, n4)
                    if not is_a:
                        second_part()
                    if not (isinstance(u, int) and u == 0 and i < 2) and (is_a or live(2)):
                        act.wait_ge(S.var, s - 1)
                        act.activation(y0[:, 0:5], var[:, 0:5], ACT.Ln).then_inc(S.ln, 1)
                        act.wait_ge(S.ln, s - 1)
                        act.activation(y0[:, 0:5], y0[:, 0:5], ACT.Exp, scale=-0.5).then_inc(S.y0, 1)
                    if live(0) and i == 1:
                        split_next((5, 6, 7))
                    if is_a:
                        second_part()
                    if live(3):
                        act.wait_ge(S.tr, n3 + 1)
                        if is_a:
                            act.activation(kT[:, :, :, i3 * P:(i3 + 1) * P].rearrange("p a b t -> p (a b) t"),
                                           ps_t[:, 0:512].rearrange("p (g t) -> p g t", t=P), ACT.Copy)
                            act.activation(qT[:, i3 % 2, 0:256], ps_t[:, 512:768], ACT.Copy).then_inc(S.qkT, 1)
                        else:
                            act.activation(qT[:, i3 % 2, :], ps_t[:, 0:512], ACT.Copy).then_inc(S.qkT, 1)
                    if live(5):
                        act.wait_ge(S.pv, n5 + 1)
                        at_least(act, S.oadd, n5)
                        if is_a:
                            act.activation(ol[:, 0:P], ps_o[:, i5 % 2, P:256], ACT.Copy).then_inc(S.ol, 1)
                        else:
                            for g in range(2):
                                src = ps_o[:, g, :].rearrange("p (j c) -> p j c", c=256)[:, :, g * P + HD:g * P + P]
                                last = act.activation(ol[:, g * P:(g + 1) * P].rearrange("p (j c) -> p j c", c=HD),
                                                      src, ACT.Copy)
                            last.then_inc(S.ol, 1)
                    if live(2):
                        act.wait_ge(S.qn, n2 + 1)
                        at_least(act, S.tr, n2)
                        act.activation(split[:, :].rearrange("p (g c) -> p g c", c=192)[:, :, 0:HD],
                                       qn[:, :].rearrange("p (g c) -> p g c", c=HD), ACT.Copy).then_inc(S.shi, 1)
                    if is_a and live(4):
                        if i4 == 0:
                            at_least(act, S.pv, n4)
                        act.activation(vs[:, i4, 0:P], stage[:, i4 % 4, 256:384], ACT.Copy).then_inc(S.vhi, 1)
                    if live(0) and i == 0:
                        split_next((0, 1))
                    if live(4):
                        act.wait_ge(S.pt, n4 + 1)
                        if is_a:
                            nk = (i4 + 1) * P
                            for c0 in range(0, nk, 512):
                                c1 = min(c0 + 512, nk)
                                last = act.activation(p_hi[:, c0:c1], ps_t[:, c0:c1], ACT.Copy)
                        else:
                            for g in range(2):
                                w0 = P if i4 == 0 else 0
                                o, src = (v[:, g * 512:(g + 1) * 512].rearrange("p (j c) -> p j c", c=256)[:, :, w0:256]
                                          for v in (p_hi, ps_t))
                                last = act.activation(o, src, ACT.Copy)
                        last.then_inc(S.phi, 1)
                    if live(0) and i == 0:
                        split_next((2, 3))
                    if not live(0) and i < 4:
                        for c in (2 * i, 2 * i + 1):
                            split_hi(units + u0, c, u_hi[:, c, 0:FW], 8 * (units + v0))
                pipeline(act, 8, units, 6, slot)

            def output(n0, u0, free_at, after_first):
                def slot(blk, i, live):
                    if live(0):
                        n = 2 * blk + i + n0
                        act.wait_ge(c_tr, n + 1)
                        at_least(act, c_mm, 2 * (n - 2) + 2)
                        for g in range(2):
                            last = act.activation(oT[:, 2 * i, g * 512:(g + 1) * 512], ps_t[:, g * 512:(g + 1) * 512],
                                                  ACT.Copy)
                        last.then_inc(c_hi, 1)
                        if isinstance(blk, int) and blk == 0 and i == 0:
                            for c in range(KD):
                                split_hi(u0 + 1, c, u_hi[:, c, FW:2 * FW], free_at)
                    if isinstance(blk, int) and blk == 0 and i == 1:
                        after_first()
                pipeline(act, 2, NT // 2, 1, slot)

            nc.scalar.preload_act_table_set("natural_log_exp_and_others")
            act.wait_ge(s_par, 16)
            act.activation(cexp[:, :], prm[:, C_VEC:C_VEC + KD], ACT.Exp, scale=-1.0).then_inc(s_cexp, 1)
            act.wait_ge(s_lam, 2)
            act.activation(lamt[:, 2:4], lamt[:, 0:2], ACT.Exp).then_inc(s_cexp, 1)
            act.wait_ge(s_mod, 3)
            act.wait_ge(bias_a, 1)
            norm(0, False)
            attn(a, A_HEADS, 0, 0, True)

            def kv_weights():
                for c in range(KD):
                    split_hi(U_KV, c, w_hi[:, c, 0:256], 8 * V_KV, 256)

            output(0, U_OUT_A, 8 * A_HEADS, kv_weights)
            act.wait_ge(s_mod, 5 + A_HEADS)
            norm(NT, True)
            attn(b, B_UNITS, V_B, U_B, False)
            output(NT, U_OUT_B, 8 * (V_B + B_UNITS), lambda: None)

        @block.vector
        def _(dve):
            def split_lo(unit, c, dst, hi, width=FW, step=1, done=w_lo_done):
                dve.wait_ge(w_hi_done, 8 * unit + c + 1)
                dve.tensor_tensor(dst, raw[:, c, 0:width], hi.bitcast(F32), ALU.subtract).then_inc(done, step)

            def newton(v, y, w, sem_y0, y0_at, step, step_at, out_rs, sem_rs):
                dve.wait_ge(sem_y0, y0_at)
                dve.tensor_tensor(ysq[:, w], y, y, ALU.mult).then_inc(step, 1)
                dve.wait_ge(step, step_at + 1)
                dve.scalar_tensor_tensor(out=yh[:, w], in0=ysq[:, w], scalar=-0.5, in1=v, op0=ALU.mult,
                                         op1=ALU.mult).then_inc(step, 1)
                dve.wait_ge(step, step_at + 2)
                dve.scalar_tensor_tensor(out=out_rs, in0=yh[:, w], scalar=1.5, in1=y, op0=ALU.add,
                                         op1=ALU.mult).then_inc(sem_rs, 1)

            def modulate(src, dst, k, shift, last_sem):
                for d in range(4):
                    last = dve.tensor_scalar(dst(d), src[:, d * P:(d + 1) * P], smod[:, k, d:d + 1],
                                             mod[:, shift + d:shift + d + 1], ALU.mult, ALU.add)
                last.then_inc(last_sem, 1)

            def norm(n0, with_kv):
                def slot(blk, i, live):
                    s = 4 * blk + i
                    n, n1, n3 = s + n0, s - 1, s - 3
                    keys = with_kv and live(3)
                    if live(0):
                        dve.wait_ge(n_ss, n + 1)
                        dve.tensor_scalar(var[:, 0:1], ssum[:, 0:1], 1.0 / D, EPS, ALU.mult, ALU.add).then_inc(n_var, 1)
                    if keys:
                        dve.wait_ge(k_raw, n3 + 1)
                        at_least(dve, k_split, n3)
                        dve.tensor_tensor(sq[:, 0:P], ol[:, 0:P], ol[:, 0:P], ALU.mult).then_inc(k_sq, 1)
                    if live(1):
                        src = (ps_t, ps_s)[(i - 1) % 2]
                        if n0 and isinstance(blk, int) and blk == 0 and i == 1:
                            dve.wait_ge(c_sum, NT)
                        dve.wait_ge(n_tr, n1 + n0 + 1)
                        at_least(dve, u_ready, n1 + n0)
                        modulate(src, lambda d: e1[:, d * P:(d + 1) * P], 2 if with_kv else 0,
                                 M_B_SHIFT if with_kv else M_A_SHIFT, n_umod_d)
                    if keys:
                        dve.wait_ge(k_sq, n3 + 1)
                        dve.tensor_reduce(ssum[:, 4:6], sq[:, 0:P].rearrange("p (g c) -> p g c", c=HD), AX.X,
                                          ALU.add).then_inc(k_sum, 1)
                    if with_kv and live(1):
                        at_least(dve, k_lo, n1)
                        modulate(src, lambda d: stage[:, 2, d * P:(d + 1) * P], 1, M_KV_SHIFT, k_umod_d)
                    if keys:
                        dve.wait_ge(k_sum, n3 + 1)
                        dve.tensor_scalar(var[:, 4:6], ssum[:, 4:6], 1.0 / HD, EPS, ALU.mult, ALU.add).then_inc(k_var, 1)
                    if live(0):
                        at_least(dve, n_norm, n)
                        newton(var[:, 0:1], y0[:, 0:1], slice(0, 1), n_y0, n + 1, n_step, 3 * n, rs[:, 0:1], n_step)
                        dve.wait_ge(n_step, 3 * n + 3)
                        dve.tensor_scalar(e0[:, i % 2, :], e0[:, i % 2, :], rs[:, 0:1], None,
                                          ALU.mult).then_inc(n_norm, 1)
                    if keys:
                        newton(var[:, 4:6], y0[:, 4:6], slice(4, 6), k_y0, n3 + 1, k_step, 3 * n3, rs[:, 4:6], k_step)
                        dve.wait_ge(k_step, 3 * n3 + 3)
                        for g in range(2):
                            last = dve.scalar_tensor_tensor(out=qn[:, g * HD:(g + 1) * HD], in0=ol[:, g * HD:(g + 1) * HD],
                                                            scalar=rs[:, 4 + g:5 + g],
                                                            in1=prm[:, C_KVK + g * HD:C_KVK + (g + 1) * HD],
                                                            op0=ALU.mult, op1=ALU.mult)
                        last.then_inc(k_kn, 1)
                    if live(1):
                        dve.wait_ge(n_hi, n1 + n0 + 1)
                        dve.tensor_tensor(u_lo[:, :, bass.ds(n1 * P, P)], e1[:, :].rearrange("p (d t) -> p d t", t=P),
                                          u_hi[:, :, bass.ds(n1 * P, P)].bitcast(F32), ALU.subtract).then_inc(u_ready, 1)
                    if not n0 and isinstance(blk, int) and blk == 0 and i < DVE_LO:
                        split_lo(0, i, w_lo[:, i, :], w_hi[:, i, :], step=8 - i if i == DVE_LO - 1 else 1)
                    if keys:
                        dve.wait_ge(k_shi, n3 + 1)
                        sp3 = split[:, 0:384].rearrange("p (g c) -> p g c", c=192)
                        dve.tensor_copy(sp3[:, :, 2 * HD:3 * HD], sp3[:, :, 0:HD].bitcast(F32))
                        dve.tensor_tensor(sp3[:, :, HD:2 * HD], qn[:, 0:P].rearrange("p (g c) -> p g c", c=HD),
                                          sp3[:, :, 0:HD].bitcast(F32), ALU.subtract).then_inc(k_split, 1)
                    if with_kv and live(1):
                        dve.wait_ge(k_hi, n1 + 1)
                        dve.tensor_tensor(p_lo[:, :], stage[:, 2:4, :].rearrange("p a n -> p (a n)"),
                                          p_hi[:, :].bitcast(F32), ALU.subtract).then_inc(k_lo, 1)
                    if n0 and not live(0) and i in (1, 2):
                        for c in range(4 * i - 4, 4 * i):
                            split_lo(U_B, c, w_lo[:, c, :], w_hi[:, c, :], step=8 - c if c == DVE_LO - 1 else 1,
                                     done=w_lo_done if c < DVE_LO else w_lo_pool)
                pipeline(dve, 4, NT // 4, 3, slot)

            def gate_columns(col, y_done):
                at_least(dve, c_sum, y_done)
                at_least(dve, c_st[0], 8 * y_done)
                at_least(dve, c_st[1], 8 * y_done)
                dve.tensor_copy(adabuf[:, 0:D].rearrange("p (d t) -> p d t", t=P),
                                mod[:, col:col + KD].unsqueeze(2).to_broadcast([P, KD, P])).then_inc(g_cols, 1)

            def gate_table(k):
                dve.wait_ge(g_mm, k + 1)
                for g in range(2):
                    last = dve.tensor_copy(e1[:, g * 512:(g + 1) * 512], ps_s[:, g * 512:(g + 1) * 512])
                last.then_inc(g_tab, 1)

            def attn(S, units, u0, is_a, gate, gate_col, y_done):
                zw = P if is_a else 256

                def masked_max(part, it, n):
                    at_least(dve, S.pt, n - 1)
                    dve.wait_ge(S.s, 2 * n + part + 1)
                    stand_alone(dve, dve_passed)
                    if is_a:
                        nk = (it + 1) * P
                        base = score_base(it)
                        e = e0[:, it % 2, 0:nk] if part == 0 else e1[:, 0:nk]
                        dve.tensor_tensor_reduce(e, ps_s[:, base:base + nk], bias[:, 1024 - nk:1024], -1.0, HUGE,
                                                 ALU.add, ALU.min, negm[:, it % 2, part:part + 1]).then_inc(S.m, 1)
                    else:
                        w0 = P if it == 0 else 0
                        for j in (2 * part, 2 * part + 1):
                            t = slice(j * 256 + w0, j * 256 + 256)
                            last = dve.tensor_tensor_reduce(e0[:, it % 2, t], ps_s[:, t], bias[:, t], -1.0,
                                                            nsink[:, j:j + 1], ALU.add, ALU.min,
                                                            negm[:, it % 2, j:j + 1])
                        last.then_inc(S.m, 1)

                def slot(u, i, live):
                    s = 8 * u + i
                    n2, n3, n4, n5, n6 = s - 2, s - 3, s - 4, s - 5, s - 6
                    i2, i4, i5, i6 = (i - 2) % 8, (i - 4) % 8, (i - 5) % 8, (i - 6) % 8
                    first = isinstance(u, int) and u == 0
                    stats = not (first and i < 2) and (is_a or live(2))

                    def split_next(chunks):
                        if first:
                            return
                        for c in chunks:
                            split_lo(u + u0, c, w_lo[:, c, :], w_hi[:, c, :], step=8 - c if c == DVE_LO - 1 else 1)

                    def normalise():
                        if stats:
                            if live(3):
                                at_least(dve, S.qn, n2)
                            if is_a:
                                at_least(dve, S.fin, n6)
                            newton(var[:, 0:5], y0[:, 0:5], slice(0, 5), S.y0, s - 1, S.step, 2 * (s - 2), rs[:, 0:5], S.rs)
                        if live(2):
                            dve.wait_ge(S.rs, s - 1)
                            dve.wait_ge(S.staged, n2 + 1)
                            at_least(dve, S.split, n2)
                            g0 = C_AQK if is_a else C_BQ
                            for g in range(4):
                                t = slice(g * HD, (g + 1) * HD)
                                last = dve.scalar_tensor_tensor(out=qn[:, t], in0=stage[:, i2 % 4, t],
                                                                scalar=rs[:, g:g + 1],
                                                                in1=prm[:, g0 + g * HD:g0 + (g + 1) * HD],
                                                                op0=ALU.mult, op1=ALU.mult)
                            last.then_inc(S.qn, 1)

                    def finish():
                        if live(6):
                            dve.wait_ge(S.zg, n6 + 1)
                            o, z = ob[:, i6 % 2, :], zs[:, i6, :]
                            if is_a:
                                dve.wait_ge(S.rs, s - 1)
                                dve.scalar_tensor_tensor(out=o[:, 0:P], in0=o[:, 0:P], scalar=rs[:, 4:5], in1=z[:, 0:P],
                                                         op0=ALU.mult, op1=ALU.mult).then_inc(S.fin, 1)
                            else:
                                dve.wait_ge(S.oadd, n6 + 1)
                                dve.wait_ge(S.ratio, 2 * n6 + 2)
                                for j in range(4):
                                    t = slice(j * HD, (j + 1) * HD)
                                    last = dve.scalar_tensor_tensor(out=o[:, t], in0=o[:, t], scalar=rl[:, i6 % 4, j:j + 1],
                                                                    in1=z[:, t], op0=ALU.mult, op1=ALU.mult)
                                last.then_inc(S.fin, 1)

                    def gate_reciprocal():
                        if live(2):
                            dve.wait_ge(S.z1, n2 + 1)
                            dve.reciprocal(ez[:, i2 % 2, 0:zw], ez[:, i2 % 2, 0:zw]).then_inc(S.zr, 1)

                    def low_probabilities(n, it):
                        dve.wait_ge(S.phi, n + 1)
                        if is_a:
                            nk = (it + 1) * P
                            for c0 in range(0, nk, 512):
                                c1 = min(c0 + 512, nk)
                                last = dve.tensor_tensor(p_lo[:, c0:c1], ps_t[:, c0:c1], p_hi[:, c0:c1].bitcast(F32),
                                                         ALU.subtract)
                        else:
                            w0 = P if it == 0 else 0
                            for g in range(2):
                                o, src, hi = (v[:, g * 512:(g + 1) * 512].rearrange("p (j c) -> p j c", c=256)[:, :, w0:256]
                                              for v in (p_lo, ps_t, p_hi))
                                last = dve.tensor_tensor(o, src, hi.bitcast(F32), ALU.subtract)
                        last.then_inc(S.plo, 1)

                    def output_sum():
                        if live(5):
                            dve.wait_ge(S.ol, n5 + 1)
                            at_least(dve, S.st[i5 % 2], 16 * (4 * (u + (i - 5) // 8) + i5 // 2))
                            if is_a:
                                dve.tensor_tensor(ob[:, i5 % 2, 0:P], ps_o[:, i5 % 2, 0:P], ol[:, 0:P],
                                                  ALU.add).then_inc(S.oadd, 1)
                                if i == 1 and live(9):
                                    dve.wait_ge(ada_mm, u)
                                    c0 = ADA0 // P + (ADAW // P) * (u - 1)
                                    dve.tensor_tensor(mod[:, bass.ds(c0, ADAW // P)],
                                                      ps_o[:, (i5 - 1) % 2, 500:500 + ADAW // P],
                                                      prm[:, bass.ds(c0 + C_ADAB, ADAW // P)], ALU.add).then_inc(s_mod, 1)
                                dve.wait_ge(S.oadd, n5 + 1)
                                at_least(dve, S.var, s - 1)
                                stand_alone(dve, dve_passed)
                                dve.tensor_tensor_reduce(junk[:, :], ob[:, i5 % 2, 0:P], ob[:, i5 % 2, 0:P], 1.0, 0.0,
                                                         ALU.mult, ALU.add, oss[:, :]).then_inc(S.oss, 1)
                            else:
                                for g in range(2):
                                    src = ps_o[:, g, :].rearrange("p (j c) -> p j c", c=256)[:, :, g * P:g * P + HD]
                                    t = slice(g * P, (g + 1) * P)
                                    last = dve.tensor_tensor(ob[:, i5 % 2, t].rearrange("p (j c) -> p j c", c=HD), src,
                                                             ol[:, t].rearrange("p (j c) -> p j c", c=HD), ALU.add)
                                last.then_inc(S.oadd, 1)

                    def second_part():
                        if live(4):
                            if is_a:
                                at_least(dve, S.comb, n4)
                            masked_max(1, i4, n4)
                            if not is_a:
                                at_least(dve, S.ratio, 2 * n4)
                                dve.wait_ge(S.m, 2 * n4 + 2)
                                dve.tensor_tensor(esnk[:, :], negm[:, i4 % 2, :], nsink[:, :], ALU.subtract).then_inc(b_snk, 1)

                    if live(4) and i == 4 and not first:
                        at_least(dve, S.m, 2 * n4)
                        dve.tensor_scalar(bias[:, :], bias[:, :], 0.5, None, ALU.mult).then_inc(S.tab, 1)
                        if not is_a:
                            dve.wait_ge(b_snk, n4)
                            dve.tensor_scalar(nsink[:, :], prm[:, bass.ds(4 * u + C_SINK, 4)], -1.0, None,
                                              ALU.mult).then_inc(b_nsink, 1)
                            dve.wait_ge(b_nsink, u + 1)
                        dve.wait_ge(S.tab, u)
                    if live(4):
                        masked_max(0, i4, n4)
                    if is_a and i4 == 0 and live(0) and live(5):
                        low_probabilities(n5, i5)
                    if not is_a:
                        second_part()
                    if live(2):
                        dve.wait_ge(S.sq, n2 + 1)
                        at_least(dve, S.var, s - 2)
                        dve.tensor_reduce(ssum[:, 0:4], sq[:, :].rearrange("p (g c) -> p g c", c=HD), AX.X,
                                          ALU.add).then_inc(S.ssum, 1)
                    if stats:
                        at_least(dve, S.rs, s - 2)
                        if live(6) and is_a:
                            dve.wait_ge(S.oss, n6 + 1)
                            dve.wait_ge(S.ratio, 3 * n6 + 2)
                            last = dve.scalar_tensor_tensor(out=var[:, 4:5], in0=oss[:, :], scalar=1.0 / P,
                                                            in1=l1e[:, i6 % 2:i6 % 2 + 1], op0=ALU.mult, op1=ALU.add)
                        if live(2):
                            dve.wait_ge(S.ssum, n2 + 1)
                            last = dve.tensor_scalar(var[:, 0:4], ssum[:, 0:4], 1.0 / HD, EPS, ALU.mult, ALU.add)
                        if not live(2) and not (live(6) and is_a):
                            last = dve.tensor_copy(junk[:, 0:1], ones[:, :])
                        last.then_inc(S.var, 1)
                    if live(0) and i == 1:
                        split_next((2, 3))
                    if is_a and i4 > 4:
                        gate_reciprocal()
                    if is_a:
                        second_part()
                    if not is_a:
                        finish()
                    normalise()
                    if not live(0) and i == 4:
                        gate_table(gate)
                    if live(4) and is_a:
                        dve.wait_ge(S.e, 2 * n4 + 2)
                        at_least(dve, S.ratio, 3 * n4)
                        at_least(dve, S.comb, n4)
                        if live(6):
                            at_least(dve, S.var, s - 1)
                        l = lsum[:, i4 % 4, :]
                        dve.reciprocal(rl[:, 0, 0:1], l[:, 1:2]).then_inc(S.ratio, 1)
                        dve.scalar_tensor_tensor(out=l1e[:, i4 % 2:i4 % 2 + 1], in0=l[:, 0:1], scalar=EPS, in1=l[:, 0:1],
                                                 op0=ALU.mult, op1=ALU.mult).then_inc(S.ratio, 1)
                        dve.wait_ge(S.ratio, 3 * n4 + 1)
                        dve.scalar_tensor_tensor(out=rl[:, 1, 0:1], in0=rl[:, 0, 0:1], scalar=lamt[:, 6:7],
                                                 in1=l[:, 0:1], op0=ALU.mult, op1=ALU.mult).then_inc(S.ratio, 1)
                        dve.wait_ge(S.ratio, 3 * n4 + 3)
                        nk = (i4 + 1) * P
                        dve.scalar_tensor_tensor(out=e0[:, i4 % 2, 0:nk], in0=e1[:, 0:nk], scalar=rl[:, 1, 0:1],
                                                 in1=e0[:, i4 % 2, 0:nk], op0=ALU.mult, op1=ALU.add).then_inc(S.comb, 1)
                    if live(4) and not is_a:
                        dve.wait_ge(b_esnk, n4 + 1)
                        dve.wait_ge(S.e, 2 * n4 + 2)
                        dve.tensor_tensor(lsum[:, i4 % 4, :], lsum[:, i4 % 4, :], esnk[:, :], ALU.add).then_inc(S.ratio, 1)
                        dve.wait_ge(S.ratio, 2 * n4 + 1)
                        dve.reciprocal(rl[:, i4 % 4, :], lsum[:, i4 % 4, :]).then_inc(S.ratio, 1)
                    output_sum()
                    if live(2):
                        dve.wait_ge(S.shi, n2 + 1)
                        sp3 = split[:, :].rearrange("p (g c) -> p g c", c=192)
                        if is_a:
                            dve.tensor_copy(sp3[:, 2:4, 2 * HD:3 * HD], sp3[:, 2:4, 0:HD].bitcast(F32))
                        dve.tensor_tensor(sp3[:, :, HD:2 * HD], qn[:, :].rearrange("p (g c) -> p g c", c=HD),
                                          sp3[:, :, 0:HD].bitcast(F32), ALU.subtract).then_inc(S.split, 1)
                    if is_a:
                        finish()
                        if i4 <= 4:
                            gate_reciprocal()
                    if live(0) and i == 0:
                        split_next((0, 1))
                    if live(4) and not (is_a and i4 == 7 and live(0)):
                        low_probabilities(n4, i4)
                    if not is_a:
                        gate_reciprocal()
                    if not live(0) and i == 2:
                        gate_columns(gate_col, y_done)
                    if not live(0) and i < 4:
                        for c in (2 * i, 2 * i + 1):
                            split_lo(units + u0, c, u_lo[:, c, 0:FW], u_hi[:, c, 0:FW])
                pipeline(dve, 8, units, 6, slot)

            def output(n0, u0, k, after_first):
                def slot(blk, i, live):
                    if live(0):
                        n = 2 * blk + i + n0
                        dve.wait_ge(c_hi, n + 1)
                        for g in range(2):
                            t = slice(g * 512, (g + 1) * 512)
                            last = dve.tensor_tensor(oT[:, 2 * i + 1, t], ps_t[:, t], oT[:, 2 * i, t].bitcast(F32),
                                                     ALU.subtract)
                        last.then_inc(c_lo, 1)
                        if isinstance(blk, int) and blk == 0 and i == 0:
                            for c in range(KD):
                                split_lo(u0 + 1, c, u_lo[:, c, FW:2 * FW], u_hi[:, c, FW:2 * FW])
                    if live(1):
                        n = 2 * blk + i - 1 + n0
                        j = (i - 1) % 2
                        if isinstance(blk, int) and blk == 0:
                            dve.wait_ge(g_tab, k + 1)
                        if n0 or not (isinstance(blk, int) and blk == 0):
                            at_least(dve, c_st[j], 16 * (blk + n0 // 2 - (0 if j == 0 else 1)))
                        for half in range(2):
                            dve.wait_ge(c_mm, 2 * n + half + 1)
                            t = slice(half * FW, (half + 1) * FW)
                            dve.tensor_tensor(adabuf[:, j * D + half * FW:j * D + (half + 1) * FW],
                                              (ps_p, ps_o)[j][:, half, :], e1[:, t], ALU.mult).then_inc(c_y, 1)
                    if isinstance(blk, int) and blk == 0 and i == 1:
                        after_first()
                pipeline(dve, 2, NT // 2, 1, slot)

            dve.memset(ones[:, :], 1.0)
            dve.memset(var[:, :], 1.0).then_inc(s_const, 1)
            dve.wait_ge(s_par, 16)
            dve.wait_ge(s_cexp, 1)
            dve.tensor_scalar(cexp[:, :], cexp[:, :], 1.0, None, ALU.add).then_inc(s_lam, 1)
            dve.tensor_scalar(prm[:, C_AQK:C_AQK + 2 * HD], prm[:, C_AQK:C_AQK + 2 * HD], HD ** -0.5, None, ALU.mult)
            dve.tensor_scalar(prm[:, C_BQ:C_BQ + 4 * HD], prm[:, C_BQ:C_BQ + 4 * HD], HD ** -0.5, None,
                              ALU.mult).then_inc(s_const, 1)
            dve.tensor_scalar(prm[:, C_SUB:C_SUB + P], prm[:, C_SUB:C_SUB + P], 1.0 - LAMBDA_INIT, None,
                              ALU.mult).then_inc(s_const, 1)
            dve.tensor_scalar(nsink[:, :], prm[:, C_SINK:C_SINK + 4], -1.0, None, ALU.mult).then_inc(b_nsink, 1)
            for k in range(2):
                c = C_LAM + 2 * k * HD
                last = dve.tensor_tensor_reduce(junk[:, k * HD:(k + 1) * HD], prm[:, c:c + HD], prm[:, c + HD:c + 2 * HD],
                                                1.0, 0.0, ALU.mult, ALU.add, lamt[:, k:k + 1])
            last.then_inc(s_lam, 1)
            dve.wait_ge(s_lam, 2)
            dve.reciprocal(csil[:, :], cexp[:, :]).then_inc(s_lam, 1)
            dve.wait_ge(s_lam, 3)
            dve.tensor_tensor(csil[:, :], csil[:, :], prm[:, C_VEC:C_VEC + KD], ALU.mult).then_inc(s_lam, 1)
            dve.wait_ge(s_cexp, 2)
            dve.tensor_tensor(lamt[:, 4:5], lamt[:, 2:3], lamt[:, 3:4], ALU.subtract).then_inc(s_lam, 1)
            dve.wait_ge(s_lam, 5)
            dve.tensor_scalar(lamt[:, 6:7], lamt[:, 4:5], LAMBDA_INIT, -1.0, ALU.add, ALU.mult).then_inc(s_lam, 1)
            dve.wait_ge(s_lam, 6)

            big = [e0[:, :, :].rearrange("p a n -> p (a n)"), stage[:, :, :].rearrange("p a n -> p (a n)")]
            for c in range(KD):
                dve.wait_ge(ada0_loaded[c % 2], 16 * (c // 2 + 1))
                if c == 0:
                    dve.tensor_scalar(adabuf[:, 0:ADA0], big[0], csil[:, 0:1], None, ALU.mult).then_inc(ada0_used, 1)
                else:
                    dve.wait_ge(ada0_used, c)
                    dve.scalar_tensor_tensor(out=adabuf[:, 0:ADA0], in0=big[c % 2], scalar=csil[:, c:c + 1],
                                             in1=adabuf[:, 0:ADA0], op0=ALU.mult, op1=ALU.add).then_inc(ada0_used, 1)
            dve.memset(junk[:, 0:1], 0.0).then_inc(s_const, 1)
            dve.wait_ge(ada0_mm, 1)
            dve.tensor_tensor(mod[:, 0:ADA0 // P], ps_p[:, 0, 0:ADA0 // P], prm[:, C_ADAB:C_ADAB + ADA0 // P],
                              ALU.add).then_inc(s_mod, 1)
            dve.wait_ge(s_mod, 1)
            dve.scalar_tensor_tensor(out=smod[:, 0, :], in0=mod[:, M_A_SCALE:M_A_SCALE + KD], scalar=1.0,
                                     in1=prm[:, C_GA:C_GA + KD], op0=ALU.add, op1=ALU.mult).then_inc(s_mod, 2)
            dve.wait_ge(s_mod, 3)
            dve.wait_ge(bias_a, 1)
            norm(0, False)
            attn(a, A_HEADS, 0, True, 0, M_A_GATE, 0)
            dve.wait_ge(s_mod, 3 + A_HEADS)
            dve.scalar_tensor_tensor(out=smod[:, 1, :], in0=mod[:, M_KV_SCALE:M_KV_SCALE + KD], scalar=1.0,
                                     in1=prm[:, C_GKV:C_GKV + KD], op0=ALU.add, op1=ALU.mult).then_inc(s_mod, 1)
            dve.scalar_tensor_tensor(out=smod[:, 2, :], in0=mod[:, M_B_SCALE:M_B_SCALE + KD], scalar=1.0,
                                     in1=prm[:, C_GB:C_GB + KD], op0=ALU.add, op1=ALU.mult).then_inc(s_mod, 1)

            def kv_weights():
                for c in range(KD):
                    split_lo(U_KV, c, w_lo[:, c, 0:256], w_hi[:, c, 0:256], 256)

            output(0, U_OUT_A, 0, kv_weights)
            dve.wait_ge(s_mod, 5 + A_HEADS)
            norm(NT, True)
            dve.wait_ge(bias_b, 1)
            attn(b, B_UNITS, U_B, False, 1, M_B_GATE, NT)
            output(NT, U_OUT_B, 1, lambda: None)


def kernel(**inputs):
    import concourse.bacc as bacc
    from concourse.bass_utils import run_bass_kernel_spmd

    f = {k: np.asarray(v) for k, v in inputs.items()}
    col = lambda v: v.reshape(-1, P).T
    row = lambda v: np.broadcast_to(v.reshape(1, -1), (P, v.size))
    units = lambda w: w.reshape(KD, P, -1, FW).transpose(2, 1, 0, 3)

    ada_b = np.concatenate([f["a_ada_b"][0], f["kv_ada_b"], f["b_ada_b"][0]])
    heads = np.arange(B_HEADS).reshape(2, B_UNITS, 2).transpose(1, 0, 2).reshape(-1)
    par = np.concatenate([
        col(f["c"][0]), col(ada_b), col(f["a_norm_g"][0]), col(f["kv_norm_g"]), col(f["b_norm_g"][0]),
        row(f["a_q_norm_g"][0]), row(f["a_q_norm_g"][0]), row(f["a_k_norm_g"][0]), row(f["a_k_norm_g"][0]),
        row(f["a_subln_g"][0]), row(f["kv_k_norm_g"]), row(f["kv_k_norm_g"]),
        *[row(f["b_q_norm_g"][0])] * 4, row(f["b_sinks"][0][heads]),
        row(f["a_lambda_q1"][0]), row(f["a_lambda_k1"][0]), row(f["a_lambda_q2"][0]), row(f["a_lambda_k2"][0]),
    ], axis=1)
    ada_w = np.concatenate([f["a_ada_w"][0], f["kv_ada_w"], f["b_ada_w"][0]], axis=1)
    ada0_w = ada_w[:, :ADA0].reshape(KD, P, ADA0)
    ada1_w = ada_w[:, ADA0:].reshape(KD, P, A_HEADS, ADAW).transpose(2, 0, 1, 3)
    wa_in = f["a_w_in"][0].reshape(D, 4, A_HEADS, P).transpose(0, 2, 1, 3).reshape(D, 4 * D)
    w_a = np.concatenate([units(wa_in), units(f["a_w_out"][0])])
    wb_in = f["b_w_in"][0].reshape(D, 2, B_HEADS, HD)[:, :, heads].reshape(D, 2, B_UNITS, 256)
    wb_in = wb_in.transpose(0, 2, 1, 3).reshape(D, 2 * D)
    wb_out = f["b_w_out"][0].reshape(B_HEADS, HD, D)[heads].reshape(D, D)
    w_b = np.concatenate([units(wb_in), units(wb_out)])
    w_kv = f["w_kv"].reshape(KD, P, 256).transpose(1, 0, 2)
    arrays = {"x": f["x"][0], "par": par, "ada0_w": ada0_w, "ada1_w": ada1_w, "w_a": w_a, "w_kv": w_kv, "w_b": w_b}
    arrays = {k: np.ascontiguousarray(v) for k, v in arrays.items()}

    nc = bacc.Bacc("TRN2", target_bir_lowering=False, num_devices=1)
    args = [nc.dram_tensor(k, v.shape, F32, kind="ExternalInput").ap() for k, v in arrays.items()]
    args.append(nc.dram_tensor("h_out", (SEQ, D), F32, kind="ExternalOutput").ap())
    build(nc, *args)
    r = run_bass_kernel_spmd(nc, [arrays], core_ids=[0])
    return r.results[0]["h_out"].reshape(f["x"].shape)
```
